# Optimizing a Trainium2 kernel written in Bass

```python
import jax, jax.numpy as jnp
from jax import lax
import numpy as np

D_MODEL = 1024
BATCH = 1
SEQ = 512
DEPTH = 2
DEC_BATCH = 8
DEC_SEQ = 1
PAST_LEN = 2048
PAGE_SIZE = 128

N_MIXERS = 2
N_HEADS = 8
QK_NOPE_DIM = 128
QK_ROPE_DIM = 64
QK_HEAD_DIM = QK_NOPE_DIM + QK_ROPE_DIM
V_HEAD_DIM = 128
Q_LORA_RANK = D_MODEL // 2
KV_LORA_RANK = D_MODEL // 4
ROPE_THETA = 10000.0
CONV_WIDTH = 3
D_FF = 2816
EPS = 1e-6
Q_BLOCK = 128
ATTN_SCALE = QK_HEAD_DIM ** -0.5

kernel_name = "hybrid_mla_shortconv_macaron_step"

def rmsnorm(x, g):
    xf = x.astype(jnp.float32)
    inv = lax.rsqrt(jnp.mean(xf * xf, axis=-1, keepdims=True) + EPS)
    return (xf * inv).astype(x.dtype) * g

def rope(x, pos):
    half = QK_ROPE_DIM // 2
    inv_freq = ROPE_THETA ** (-jnp.arange(half, dtype=jnp.float32) / half)
    ang = pos.astype(jnp.float32)[:, None] * inv_freq[None, :]
    shape = (ang.shape[0],) + (1,) * (x.ndim - 3) + (half,)
    cos = jnp.cos(ang).reshape(shape)
    sin = jnp.sin(ang).reshape(shape)
    x1 = x[..., :half].astype(jnp.float32)
    x2 = x[..., half:].astype(jnp.float32)
    return jnp.concatenate([x1 * cos - x2 * sin, x1 * sin + x2 * cos], axis=-1).astype(x.dtype)

def swiglu(h, wg, wu, wd):
    return (jax.nn.silu(h @ wg) * (h @ wu)) @ wd

def mla_project(h, pos, w_dq, q_a_norm, w_uq, w_dkv, kv_a_norm, q_norm):
    cq = rmsnorm(h @ w_dq, q_a_norm)
    q = jnp.einsum('btr,rhd->bthd', cq, w_uq)
    q = jnp.concatenate([q[..., :QK_NOPE_DIM], rope(q[..., QK_NOPE_DIM:], pos)], axis=-1)
    q = rmsnorm(q, q_norm)
    kv = h @ w_dkv
    lat = rmsnorm(kv[..., :KV_LORA_RANK], kv_a_norm)
    kr = rope(kv[..., KV_LORA_RANK:], pos)
    return q, lat, kr

def mla_keys(lat, kr, w_uk, k_norm):
    k_nope = jnp.einsum('...c,chd->...hd', lat, w_uk)
    k_rope = jnp.broadcast_to(kr[..., None, :], k_nope.shape[:-1] + (QK_ROPE_DIM,))
    return rmsnorm(jnp.concatenate([k_nope, k_rope], axis=-1), k_norm)

def mla_prompt(h, w_dq, q_a_norm, w_uq, w_dkv, kv_a_norm, q_norm, k_norm, w_uk, w_uv, w_o):
    b, s, _ = h.shape
    pos = jnp.arange(s, dtype=jnp.int32)
    q, lat, kr = mla_project(h, pos, w_dq, q_a_norm, w_uq, w_dkv, kv_a_norm, q_norm)
    k = mla_keys(lat, kr, w_uk, k_norm)
    v = jnp.einsum('bsc,chd->bshd', lat, w_uv)
    nb = s // Q_BLOCK
    kpos = jnp.arange(s, dtype=jnp.int32)

    def attend_block(args):
        qb, blk = args
        sc = jnp.einsum('bqhd,bkhd->bhqk', qb, k).astype(jnp.float32) * ATTN_SCALE
        qpos = blk * Q_BLOCK + jnp.arange(Q_BLOCK, dtype=jnp.int32)
        sc = jnp.where(kpos[None, :] <= qpos[:, None], sc, -jnp.inf)
        p = jax.nn.softmax(sc, axis=-1).astype(v.dtype)
        return jnp.einsum('bhqk,bkhd->bqhd', p, v)

    qblocks = q.reshape(b, nb, Q_BLOCK, N_HEADS, QK_HEAD_DIM).transpose(1, 0, 2, 3, 4)
    o = lax.map(attend_block, (qblocks, jnp.arange(nb, dtype=jnp.int32)))
    o = o.transpose(1, 0, 2, 3, 4).reshape(b, s, N_HEADS, V_HEAD_DIM)
    return jnp.einsum('bshv,hvd->bsd', o, w_o), lat, kr

def mla_sample(h, cache_latent, cache_krope, page_table,
               w_dq, q_a_norm, w_uq, w_dkv, kv_a_norm, q_norm, k_norm, w_uk, w_uv, w_o):
    ds = h.shape[1]
    pos = PAST_LEN + jnp.arange(ds, dtype=jnp.int32)
    q, lat_new, kr_new = mla_project(h, pos, w_dq, q_a_norm, w_uq, w_dkv, kv_a_norm, q_norm)
    kpos = jnp.arange(PAST_LEN + ds, dtype=jnp.int32)
    qpos = PAST_LEN + jnp.arange(ds, dtype=jnp.int32)
    mask = kpos[None, :] <= qpos[:, None]

    def one_seq(args):
        qs, pages, ln, kn = args
        lat_all = jnp.concatenate([cache_latent[pages].reshape(PAST_LEN, KV_LORA_RANK), ln], axis=0)
        kr_all = jnp.concatenate([cache_krope[pages].reshape(PAST_LEN, QK_ROPE_DIM), kn], axis=0)
        k = mla_keys(lat_all, kr_all, w_uk, k_norm)
        sc = jnp.einsum('qhd,khd->hqk', qs, k).astype(jnp.float32) * ATTN_SCALE
        sc = jnp.where(mask[None], sc, -jnp.inf)
        p = jax.nn.softmax(sc, axis=-1).astype(lat_all.dtype)
        o_lat = jnp.einsum('hqk,kc->qhc', p, lat_all)
        return jnp.einsum('qhc,chd->qhd', o_lat, w_uv)

    o = lax.map(one_seq, (q, page_table, lat_new, kr_new))
    return jnp.einsum('bshv,hvd->bsd', o, w_o), lat_new, kr_new

def short_conv(h, buf, w_conv_in, conv_w, w_conv_out):
    t = h.shape[1]
    bcx = h @ w_conv_in
    gb = bcx[..., :D_MODEL]
    gc = bcx[..., D_MODEL:2 * D_MODEL]
    xv = bcx[..., 2 * D_MODEL:]
    u = gc * xv
    u_ext = jnp.concatenate([buf, u], axis=1)
    y = sum(conv_w[j] * u_ext[:, j:j + t] for j in range(CONV_WIDTH))
    return (gb * y) @ w_conv_out, u_ext[:, -(CONV_WIDTH - 1):]

def setup_inputs(seed: int = 0) -> dict:
    key = jax.random.key(seed)
    ks = iter(jax.random.split(key, 40))
    f32 = jnp.float32

    def w(shape, fan_in):
        return jax.random.normal(next(ks), shape, f32) * (fan_in ** -0.5)

    def gain(shape):
        return 1.0 + 0.05 * jax.random.normal(next(ks), shape, f32)

    n_pages = PAST_LEN // PAGE_SIZE
    n_used = DEC_BATCH * n_pages
    n_pool = (n_used * 5) // 4
    x_prompt = jax.random.normal(next(ks), (BATCH, SEQ, D_MODEL), f32)
    x_sample = jax.random.normal(next(ks), (DEC_BATCH, DEC_SEQ, D_MODEL), f32)
    cache_latent = jax.random.normal(next(ks), (n_pool, PAGE_SIZE, KV_LORA_RANK), f32)
    cache_krope = jax.random.normal(next(ks), (n_pool, PAGE_SIZE, QK_ROPE_DIM), f32)
    state_conv = jax.random.normal(next(ks), (DEC_BATCH, CONV_WIDTH - 1, D_MODEL), f32)
    page_table = jax.random.permutation(next(ks), n_pool)[:n_used].reshape(DEC_BATCH, n_pages).astype(jnp.int32)
    return {
        "x_prompt": x_prompt, "x_sample": x_sample,
        "cache_latent": cache_latent, "cache_krope": cache_krope, "state_conv": state_conv,
        "page_table": page_table,
        "norm_ffn1": gain((DEPTH, D_MODEL)),
        "w_ffn1_gate": w((DEPTH, D_MODEL, D_FF), D_MODEL),
        "w_ffn1_up": w((DEPTH, D_MODEL, D_FF), D_MODEL),
        "w_ffn1_down": w((DEPTH, D_FF, D_MODEL), D_FF),
        "norm_mix": gain((DEPTH, D_MODEL)),
        "norm_ffn2": gain((DEPTH, D_MODEL)),
        "w_ffn2_gate": w((DEPTH, D_MODEL, D_FF), D_MODEL),
        "w_ffn2_up": w((DEPTH, D_MODEL, D_FF), D_MODEL),
        "w_ffn2_down": w((DEPTH, D_FF, D_MODEL), D_FF),
        "w_dq": w((D_MODEL, Q_LORA_RANK), D_MODEL),
        "q_a_norm": gain((Q_LORA_RANK,)),
        "w_uq": w((Q_LORA_RANK, N_HEADS, QK_HEAD_DIM), Q_LORA_RANK),
        "w_dkv": w((D_MODEL, KV_LORA_RANK + QK_ROPE_DIM), D_MODEL),
        "kv_a_norm": gain((KV_LORA_RANK,)),
        "q_norm": gain((QK_HEAD_DIM,)),
        "k_norm": gain((QK_HEAD_DIM,)),
        "w_uk": w((KV_LORA_RANK, N_HEADS, QK_NOPE_DIM), KV_LORA_RANK),
        "w_uv": w((KV_LORA_RANK, N_HEADS, V_HEAD_DIM), KV_LORA_RANK),
        "w_o_attn": w((N_HEADS, V_HEAD_DIM, D_MODEL), N_HEADS * V_HEAD_DIM),
        "w_conv_in": w((D_MODEL, 3 * D_MODEL), D_MODEL),
        "conv_w": w((CONV_WIDTH, D_MODEL), CONV_WIDTH),
        "w_conv_out": w((D_MODEL, D_MODEL), D_MODEL),
    }

def reference(x_prompt, x_sample, cache_latent, cache_krope, state_conv, page_table,
              norm_ffn1, w_ffn1_gate, w_ffn1_up, w_ffn1_down, norm_mix, norm_ffn2,
              w_ffn2_gate, w_ffn2_up, w_ffn2_down,
              w_dq, q_a_norm, w_uq, w_dkv, kv_a_norm, q_norm, k_norm, w_uk, w_uv, w_o_attn,
              w_conv_in, conv_w, w_conv_out):
    xp, xs = x_prompt, x_sample
    mla_w = (w_dq, q_a_norm, w_uq, w_dkv, kv_a_norm, q_norm, k_norm, w_uk, w_uv, w_o_attn)
    for i in range(DEPTH):
        xp = xp + 0.5 * swiglu(rmsnorm(xp, norm_ffn1[i]), w_ffn1_gate[i], w_ffn1_up[i], w_ffn1_down[i])
        xs = xs + 0.5 * swiglu(rmsnorm(xs, norm_ffn1[i]), w_ffn1_gate[i], w_ffn1_up[i], w_ffn1_down[i])
        hp = rmsnorm(xp, norm_mix[i])
        hs = rmsnorm(xs, norm_mix[i])
        if i % N_MIXERS == 0:
            mp, lat_p, kr_p = mla_prompt(hp, *mla_w)
            ms, lat_s, kr_s = mla_sample(hs, cache_latent, cache_krope, page_table, *mla_w)
        else:
            zero_buf = jnp.zeros((hp.shape[0], CONV_WIDTH - 1, D_MODEL), hp.dtype)
            mp, conv_p = short_conv(hp, zero_buf, w_conv_in, conv_w, w_conv_out)
            ms, conv_s = short_conv(hs, state_conv, w_conv_in, conv_w, w_conv_out)
        xp = xp + mp
        xs = xs + ms
        xp = xp + 0.5 * swiglu(rmsnorm(xp, norm_ffn2[i]), w_ffn2_gate[i], w_ffn2_up[i], w_ffn2_down[i])
        xs = xs + 0.5 * swiglu(rmsnorm(xs, norm_ffn2[i]), w_ffn2_gate[i], w_ffn2_up[i], w_ffn2_down[i])
    return (xp, xs, lat_p, kr_p, conv_p, lat_s, kr_s, conv_s)


_drawn_inputs = setup_inputs


def setup_inputs(seed=0):
    import zlib

    import numpy as np

    out = dict(_drawn_inputs(seed))
    spreads = {}
    factors = {'q_a_norm': 5.504, 'q_norm': 5.68, 'k_norm': 5.401}
    for name, (base, spread) in spreads.items():
        noise = np.random.default_rng([zlib.crc32(name.encode()), seed]).standard_normal(out[name].shape)
        drawn = base * np.exp(spread * noise) if base else spread * noise
        out[name] = __import__('jax').numpy.asarray(drawn.astype(out[name].dtype))
    for name, factor in factors.items():
        out[name] = (out[name] * factor).astype(out[name].dtype)
    return out
```

```python
from contextlib import ExitStack

import numpy as np
import concourse.bass as bass
from concourse import mybir

F32 = mybir.dt.float32
F32R = mybir.dt.float32r
I32 = mybir.dt.int32
ALU = mybir.AluOpType
ACT = mybir.ActivationFunctionType
AX = mybir.AxisListType

P = 128
D = 1024
KD = D // P
SEQ = 512
QT = SEQ // P
DEC = 8
T = SEQ + DEC
HALF = T // 2
FF = 2816
NF = FF // P
H = 8
NOPE = 128
ROPE = 64
RH = ROPE // 2
HD = NOPE + ROPE
VD = 128
QR = 512
KQ = QR // P
CL = 256
KC = CL // P
PAST = 2048
PAGE = 128
PAGES = PAST // PAGE
POOL = 160
EPS = 1e-6
ATTN_SCALE = HD ** -0.5
THETA = 10000.0
NEG = -1e30
CONV = 3
RAW = 4
UC = 1024
DOWN = (8, 8, NF - 16)
NT = QT + 1
ROW = CL + 2 + ROPE
ONE = CL
KR = CL + 2


def col0(i):
    return DEC + P * i if i < QT else 0


def width(i):
    return P if i < QT else DEC


def cols(t, start, n):
    return t[:, start:start + n] if isinstance(start, int) else t[:, bass.ds(start, n)]


class Unit:

    def __init__(self, base, it=0, step=0):
        assert step % RAW == 0
        self.slot, self.half = base % RAW, base % 2
        self.n = base + step * it
        self.turn = base // RAW + (step // RAW) * it


class Chain:

    def __init__(self, eng, sem):
        self.eng, self.sem, self.n = eng, sem, 0

    def link(self, ins):
        self.n += 1
        ins.then_inc(self.sem, 1)
        self.eng.wait_ge(self.sem, self.n)


def build(nc, a, out, stages=("ffn0", "mla", "ffn1", "ffn2", "conv", "ffn3")):
    ctx = ExitStack()
    with ctx:
        def sb(name, shape, dt=F32, scope=ctx):
            return scope.enter_context(nc.sbuf_tensor(name, shape, dt))

        def sem(name):
            return ctx.enter_context(nc.semaphore(name))

        ps = ctx.enter_context(nc.psum_tensor("ps", [P, 8, 512], F32))
        xT = sb("xT", [P, KD * T])
        raw = sb("raw", [P, RAW, UC])
        w_hi = sb("w_hi", [P, 2, UC], F32R)
        w_lo = sb("w_lo", [P, 2, UC], F32R)
        ident = sb("ident", [P, P])
        ones = sb("ones", [P, P])
        gain = sb("gain", [P, 72])
        acc = sb("acc", [P, T])
        sq = sb("sq", [P, T])
        inv = sb("inv", [P, T])
        causal = sb("causal", [P, P])
        own = sb("own", [DEC, DEC, H])
        cosr = sb("cosr", [P, NT, RH])
        sinr = sb("sinr", [P, NT, RH])
        gqk = inv[:, 0:HD]
        kr = inv[:, HD:HD + NT * ROPE].rearrange("p (t c) -> p t c", t=NT)
        latnew = sb("latnew", [DEC, CL + 1])
        st = sb("st", [P, 11, NT])
        qs = sb("qs", [P, NT, H])
        rk = sb("rk", [P, NT, H])
        stat8 = sb("stat8", [P, NT, H])
        with ExitStack() as z:
            h_hi = sb("h_hi", [P, KD * T], F32R, z)
            h_lo = sb("h_lo", [P, KD * T], F32R, z)
        with ExitStack() as z:
            sqs = sb("sqs", [P, H * HD], F32, z)
            q_rope = sb("q_rope", [P, 2, H * ROPE], F32, z)
            k_rope = sb("k_rope", [P, 2, H * ROPE], F32, z)
            k_nat = sb("k_nat", [P, QT, H * NOPE], F32, z)
        ctx.enter_context(nc.sbuf_tensor("h_space", [P, 2 * KD * T], F32))

        with ExitStack() as m:
            g_hi = sb("g_hi", [P, NF * T], F32R, m)
            g_lo = sb("g_lo", [P, NF * T], F32R, m)
            gate_t = sb("gate_t", [P, T], F32, m)
            silu_t = sb("silu_t", [P, T], F32, m)
            up_t = sb("up_t", [P, T], F32, m)
            hid_t = sb("hid_t", [P, T], F32, m)
            st_nat = sb("st_nat", [2 * DEC, D], F32, m)
            stT = sb("stT", [P, KD, 2 * DEC], F32, m)
            tail = sb("tail", [P, KD, 2 + DEC], F32, m)
            tail_nat = sb("tail_nat", [2 + DEC, D], F32, m)
        with ExitStack() as m:
            x_nat = sb("x_nat", [P, QT, D], F32, m)
            xs_nat = sb("xs_nat", [DEC, D], F32, m)
            gain_rows = sb("gain_rows", [72, P], F32, m)
            y_nat = sb("y_nat", [P, 2, D], F32, m)
        with ExitStack() as m:
            z_hi = sb("z_hi", [P, KD * T], F32R, m)
            z_lo = sb("z_lo", [P, KD * T], F32R, m)
            ue = sb("ue", [P, 2, DEC + CONV - 1 + SEQ], F32, m)
            ca = sb("ca", [P, T], F32, m)
            cb = sb("cb", [P, T], F32, m)
            cg = sb("cg", [P, T], F32, m)
            cy = sb("cy", [P, T], F32, m)
            cz = sb("cz", [P, T], F32, m)
        with ExitStack() as m:
            wuk_hi = sb("wuk_hi", [P, KC, H * NOPE + H], F32R, m)
            wuk_lo = sb("wuk_lo", [P, KC, H * NOPE + H], F32R, m)
            with ExitStack() as r:
                q_n = sb("q_n", [P, H, SEQ], F32, r)
                q_r = sb("q_r", [P, H // 2, SEQ], F32, r)
            with ExitStack() as r:
                kv_nat = sb("kv_nat", [P, NT, CL + ROPE], F32, r)
                lat = sb("lat", [P, NT, CL], F32, r)
                q_row = sb("q_row", [P, QR], F32, r)
                kv_row = sb("kv_row", [P, CL], F32, r)
                kt = sb("kt", [P, 4, NT, RH], F32, r)
                gk_row = sb("gk_row", [P, HD], F32, r)
            with ExitStack() as r:
                cache1 = sb("cache1", [P, PAGES, ROW], F32, r)
            m.enter_context(nc.sbuf_tensor("q_space", [P, 3 * H // 2 * SEQ], F32))
            with ExitStack() as r:
                k_n = sb("k_n", [P, H, SEQ], F32, r)
                k_r = sb("k_r", [P, H // 2, SEQ], F32, r)
                v = sb("v", [P, QT, H * VD], F32, r)
            with ExitStack() as r:
                q_nat = sb("q_nat", [P, NT, H * HD], F32, r)
                cq_nat = sb("cq_nat", [P, NT, QR], F32, r)
            with ExitStack() as r:
                latT_hi = sb("latT_hi", [P, 2, CL], F32R, r)
                latT_lo = sb("latT_lo", [P, 2, CL], F32R, r)
                krT = sb("krT", [ROPE, 2, P], F32, r)
                ksq = sb("ksq", [P, 2, H * NOPE], F32, r)
                kss = sb("kss", [P, 2, PAGES, H], F32, r)
                sc = sb("sc", [P, 2, PAGES + 1, H], F32, r)
                pr = sb("pr", [P, 2, PAGES + 1, H], F32, r)
                krq = sb("krq", [P, PAGES, ROPE], F32, r)
                krs = sb("krs", [P, PAGES], F32, r)
                kms = sb("kms", [P, PAGES, H], F32, r)
                kinv = sb("kinv", [P, PAGES, H], F32, r)
                kroot = sb("kroot", [P, PAGES, H], F32, r)
                mx8 = sb("mx8", [P, H], F32, r)
                mxa = sb("mxa", [P, H], F32, r)
                ol = sb("ol", [DEC, CL], F32, r)
                rden = sb("rden", [DEC, 1], F32, r)
                oT = sb("oT", [P, KC, H, DEC], F32, r)
            m.enter_context(nc.sbuf_tensor("k_space", [P, (3 * H // 2 + 8) * SEQ], F32))
            with ExitStack() as r:
                cq_hi = sb("cq_hi", [P, KQ, T], F32R, r)
                cq_lo = sb("cq_lo", [P, KQ, T], F32R, r)
                lt_hi = sb("lt_hi", [P, KC, T], F32R, r)
                lt_lo = sb("lt_lo", [P, KC, T], F32R, r)
                wu_raw = sb("wu_raw", [P, KC, H * NOPE], F32, r)
            with ExitStack() as r:
                cache0 = sb("cache0", [P, PAGES, ROW], F32, r)
                pt = sb("pt", [P, QT, SEQ], F32, r)
                pn = sb("pn", [P, 2, SEQ], F32, r)
            with ExitStack() as r:
                sb("wuv_space", [P, PAGES, ROW], F32, r)
                wuv_raw = sb("wuv_raw", [P, KC, H * VD], F32, r)
            m.enter_context(nc.sbuf_tensor("late_space", [P, 6 * T * 2 + KC * H * NOPE], F32))
            qsT = sb("qsT", [P, H, DEC], F32, m)
            qrT = sb("qrT", [ROPE, DEC, H], F32, m)
            qrb = sb("qrb", [ROPE, H], F32, m)
            qa_hi = sb("qa_hi", [P, KC, DEC, H], F32R, m)
            qa_lo = sb("qa_lo", [P, KC, DEC, H], F32R, m)
            s_new = sb("s_new", [DEC, DEC, H], F32, m)
            mxp = sb("mxp", [P, QT * H], F32, m)
            nb = sb("nb", [P, QT * H], F32, m)
            sums = sb("sums", [P, QT * H], F32, m)
            rs = sb("rs", [P, QT * H], F32, m)
            kr_newT = sb("kr_newT", [ROPE, DEC], F32, m)

        weights_in = [sem(f"weights_in{i}") for i in range(RAW)]
        unit_hi_made, unit_lo_made, unit_used = sem("unit_hi_made"), sem("unit_lo_made"), sem("unit_used")
        x_in, small_in, ident_made, consts_made = sem("x_in"), sem("small_in"), sem("ident_made"), sem("consts_made")
        xt_made, gains_made, gains_T = sem("xt_made"), sem("gains_made"), sem("gains_T")
        x_ready, hh_made, sq_made = sem("x_ready"), sem("hh_made"), sem("sq_made")
        h_ready, acc_done, acc_cleared = sem("h_ready"), sem("acc_done"), sem("acc_cleared")
        stats_made, ms_made, recip_made, inv_made = sem("stats_made"), sem("ms_made"), sem("recip_made"), sem("inv_made")
        gate_scaled, silu_made, up_scaled = sem("gate_scaled"), sem("silu_made"), sem("up_scaled")
        hid_made, hid_hi_made, hid_done = sem("hid_made"), sem("hid_hi_made"), sem("hid_done")
        y_turned, y_copied, y_out = sem("y_turned"), [sem("y_copied_dve"), sem("y_copied_act")], [sem("y_out0"), sem("y_out1")]
        dve_step, act_step, pool_step = sem("dve_step"), sem("act_step"), sem("pool_step")
        stores, rows_out = sem("stores"), sem("rows_out")
        rows_in, wu_in, wuv_in, cq_nat_made, kv_nat_made = (
            sem("rows_in"), sem("wu_in"), sem("wuv_in"), sem("cq_nat_made"), sem("kv_nat_made"))
        cqn_made, latn_made, tv_made, tv_hi_made, tv_lo_made = (
            sem("cqn_made"), sem("latn_made"), sem("tv_made"), sem("tv_hi_made"), sem("tv_lo_made"))
        kr_made, job_read, turned, q_post_made, k_post_made = (
            sem("kr_made"), sem("job_read"), sem("turned"), sem("q_post_made"), sem("k_post_made"))
        rope_made, qsq_made, row_rec, row_root, ksum_made = (
            sem("rope_made"), sem("qsq_made"), sem("row_rec"), sem("row_root"), sem("ksum_made"))
        latnew_made, wuk_turned, wukT_made, qa_heads, kr_turned = (
            sem("latnew_made"), sem("wuk_turned"), sem("wukT_made"), sem("qa_heads"), sem("kr_turned"))
        kr_newT_made, qa_hi_made, qa_made, s_new_raw, s_new_read = (
            sem("kr_newT_made"), sem("qa_hi_made"), sem("qa_made"), sem("s_new_raw"), sem("s_new_read"))
        scores_made, neg_made, exp_made, pn_made, p_turned = (
            sem("scores_made"), sem("neg_made"), sem("exp_made"), sem("pn_made"), sem("p_turned"))
        pt_made, o_made, o_hi_made, o_lo_made, attn_left = (
            sem("pt_made"), sem("o_made"), sem("o_hi_made"), sem("o_lo_made"), sem("attn_left"))
        t_made, lath_made, latl_made, krt_made, k_made = (
            sem("t_made"), sem("lath_made"), sem("latl_made"), sem("krt_made"), sem("k_made"))
        squares_made, scores_copied, kss_made, query_set, krq_made = (
            sem("squares_made"), sem("scores_copied"), sem("kss_made"), sem("query_set"), sem("krq_made"))
        krs_made, kms_made, kinv_made, kroot_made, sc_scaled = (
            sem("krs_made"), sem("kms_made"), sem("kinv_made"), sem("kroot_made"), sem("sc_scaled"))
        mx_made, mxa_made, sc_ready, pr_made, pv_made = (
            sem("mx_made"), sem("mxa_made"), sem("sc_ready"), sem("pr_made"), sem("pv_made"))
        rden_made, ol_made, ol_turned, oT_made, os_made = (
            sem("rden_made"), sem("ol_made"), sem("ol_turned"), sem("oT_made"), sem("os_made"))
        os_hi_made, os_lo_made = (
            sem("os_hi_made"), sem("os_lo_made"))
        cache_in = [[sem(f"cache{i}_in{g}") for g in range(PAGES // 4)] for i in range(2)]
        cache_ones = [sem("cache_ones0"), sem("cache_ones1")]
        state_in, state_T, state_copied = sem("state_in"), sem("state_T"), sem("state_copied")
        conv_read, u_made, z_made, zh_made, z_ready = (sem("conv_read"), sem("u_made"), sem("z_made"), sem("zh_made"),
                                                       sem("z_ready"))
        tail_made, tail_T, tails_copied = sem("tail_made"), sem("tail_T"), [sem("tail_copied_act"), sem("tail_copied_dve")]

        gate_w = [a["w_ffn1_gate"][0], a["w_ffn2_gate"][0], a["w_ffn1_gate"][1], a["w_ffn2_gate"][1]]
        up_w = [a["w_ffn1_up"][0], a["w_ffn2_up"][0], a["w_ffn1_up"][1], a["w_ffn2_up"][1]]
        down_w = [a["w_ffn1_down"][0], a["w_ffn2_down"][0], a["w_ffn1_down"][1], a["w_ffn2_down"][1]]
        ALL = ("ffn0", "mla", "ffn1", "ffn2", "conv", "ffn3")
        GAIN = [ALL.index(s) for s in stages]
        FFN_NORM = [stages.index(f"ffn{i}") if f"ffn{i}" in stages else None for i in range(4)]
        MLA_NORM, CONV_NORM = (stages.index(s) if s in stages else None for s in ("mla", "conv"))
        ROW_USE = {}

        wukT = sq[:, 0:2 * CL].rearrange("p (b c) -> p b c", b=2)

        plan, u = [], 0
        NU = {"ffn": 2 * NF + 3 * KD, "mla": 26, "conv": 4 * KD}
        for s in stages:
            plan.append((s, u))
            u += NU[s.rstrip("0123")]
            if s != "mla":
                ROW_USE[FFN_NORM[int(s[-1])] if s[:3] == "ffn" else CONV_NORM] = len(ROW_USE)
        LAST_UNIT = u

        def slot(s):
            return ps[:, 2 * s:2 * s + 2, 0:HALF]

        def two(ap):
            return ap.rearrange("p (b n) -> p b n", b=2)

        def load_unit(sp, un, src, n, shape):
            if not (isinstance(un.n, int) and un.n < RAW):
                sp.wait_ge(unit_lo_made, un.n - RAW + 1)
            dst = raw[:, un.slot, 0:n].rearrange("p (k c) -> p k c", k=shape)
            sp.dma_start(dst, src).then_inc(weights_in[un.slot], 16)

        def split_hi(act, un, n=UC, dst=None):
            act.wait_ge(weights_in[un.slot], 16 * (un.turn + 1))
            if not (isinstance(un.n, int) and un.n < 2):
                act.wait_ge(unit_used, un.n - 1)
            src = raw[:, un.slot, 0:n]
            if dst is not None:
                src = src.rearrange("p (k c) -> p k c", k=KC)
            nc.scalar.copy(w_hi[:, un.half, 0:n] if dst is None else dst, src).then_inc(unit_hi_made, 1)

        def split_lo(dve, un, n=UC, dst=None):
            dve.wait_ge(unit_hi_made, un.n + 1)
            src = raw[:, un.slot, 0:n]
            if dst is None:
                nc.vector.tensor_tensor(w_lo[:, un.half, 0:n], src, w_hi[:, un.half, 0:n],
                                        ALU.subtract).then_inc(unit_lo_made, 1)
            else:
                src = src.rearrange("p (k c) -> p k c", k=KC)
                nc.vector.tensor_tensor(dst[1], src, dst[0], ALU.subtract).then_inc(unit_lo_made, 1)

        def product(s, hi, lo, mh, ml, k, start, stop):
            x0 = k * T
            o = [ps[:, 2 * s, 0:HALF], ps[:, 2 * s + 1, 0:HALF]]
            for b in range(2):
                nc.tensor.matmul(o[b], hi, mh[:, x0 + b * HALF:x0 + (b + 1) * HALF], start=start, stop=False)
            for b in range(2):
                nc.tensor.matmul(o[b], hi, ml[:, x0 + b * HALF:x0 + (b + 1) * HALF], start=False, stop=False)
            for b in range(2):
                mm = nc.tensor.matmul(o[b], lo, mh[:, x0 + b * HALF:x0 + (b + 1) * HALF], start=False, stop=stop)
            return mm

        def w_unit(un, k, n=P):
            return w_hi[:, un.half, k * n:(k + 1) * n], w_lo[:, un.half, k * n:(k + 1) * n]

        def publish_act(act, n, k):
            act.wait_ge(gains_made, 1)
            act.wait_ge(x_ready, KD * n + k + 1)
            nc.scalar.activation(cols(h_hi, k * T, T), cols(xT, k * T, T), ACT.Copy,
                                 scale=cols(gain, KD * GAIN[n] + k, 1)).then_inc(hh_made, 1)
            act.wait_ge(gains_made, 1)
            if not (n == 0 and k == 0):
                act.wait_ge(acc_done, KD * n + k)
            nc.scalar.activation(sq[:], cols(xT, k * T, T), ACT.Square).then_inc(sq_made, 1)

        def publish_dve(dve, n, k):
            dve.wait_ge(hh_made, KD * n + k + 1)
            nc.vector.scalar_tensor_tensor(out=cols(h_lo, k * T, T), in0=cols(xT, k * T, T),
                                           scalar=cols(gain, KD * GAIN[n] + k, 1), in1=cols(h_hi, k * T, T),
                                           op0=ALU.mult, op1=ALU.subtract).then_inc(h_ready, 1)
            dve.wait_ge(sq_made, KD * n + k + 1)
            dve.wait_ge(acc_cleared, n + 1)
            if not (n == 0 and k == 0):
                dve.wait_ge(acc_done, KD * n + k)
            nc.vector.tensor_tensor(acc[:], acc[:], sq[:], ALU.add).then_inc(acc_done, 1)

        def norm_pe(pe, n):
            pe.wait_ge(acc_done, KD * (n + 1))
            for b in range(2):
                mm = nc.tensor.matmul(ps[:, 6 + b, 0:HALF], ones[:], acc[:, b * HALF:(b + 1) * HALF],
                                      start=True, stop=True)
            mm.then_inc(stats_made, 1)

        def norm_dve(dve, n):
            r = ROW_USE[n]
            dve.wait_ge(stats_made, n + 1)
            if r:
                dve.wait_ge(inv_made, r)
            nc.vector.memset(acc[:], 0.0).then_inc(acc_cleared, 1)
            nc.vector.tensor_scalar(two(inv[:]), slot(3), 1.0 / D, EPS, ALU.mult, ALU.add).then_inc(ms_made, 1)
            dve.wait_ge(ms_made, r + 1)
            nc.vector.reciprocal(sq[:], inv[:]).then_inc(recip_made, 1)

        def norm_act(act, n):
            r = ROW_USE[n]
            act.wait_ge(recip_made, r + 1)
            nc.scalar.activation(inv[:], sq[:], ACT.Sqrt).then_inc(inv_made, 1)

        def ffn_sp(sp, i, u0):
            gw = gate_w[i].rearrange("(k p) f -> p k f", p=P)
            uw = up_w[i].rearrange("(k p) f -> p k f", p=P)
            dw = down_w[i].rearrange("(k p) d -> p k d", p=P)

            def gate_up(it):
                for j in range(4):
                    f = (2 * it + j // 2) * P
                    src = gw if j % 2 == 0 else uw
                    src = src[:, :, f:f + P] if isinstance(f, int) else src[:, :, bass.ds(f, P)]
                    load_unit(sp, Unit(u0 + j, it, 4), src, UC, KD)

            gate_up(0)
            with sp.Fori(1, NF // 2) as it:
                gate_up(it)
            with sp.Fori(0, 2) as it:
                for j in range(12):
                    k0 = sum(DOWN[:j % 3])
                    nk = DOWN[j % 3]
                    load_unit(sp, Unit(u0 + 2 * NF + j, it, 12),
                              dw[:, k0:k0 + nk, bass.ds((4 * it + j // 3) * P, P)], nk * P, nk)

        def ffn_pe(pe, i, u0):
            n, f0 = FFN_NORM[i], NF * FFN_AT[i]

            def gate_up(it):
                first = isinstance(it, int)
                for j in range(4):
                    un = Unit(u0 + j, it, 4)
                    pe.wait_ge(unit_lo_made, un.n + 1)
                    if first and j == 0:
                        pe.wait_ge(x_ready, KD * n + 5)
                    if first and j == 3:
                        pe.wait_ge(inv_made, ROW_USE[n] + 1)
                    if not first and j % 2 == 0:
                        pe.wait_ge(hid_done, f0 + 2 * it + j // 2 - 1)
                    for k in range(KD):
                        if first and j == 0:
                            pe.wait_ge(h_ready, KD * n + k + 1)
                        mm = product(j, *w_unit(un, k), h_hi, h_lo, k, k == 0, k == KD - 1)
                    mm.then_inc(unit_used, 1)
                    if first and j == 0:
                        norm_pe(pe, n)

            gate_up(0)
            with pe.Fori(1, NF // 2) as it:
                gate_up(it)
            with pe.Fori(0, 2) as it:
                for j in range(12):
                    m, p = j // 3, j % 3
                    un = Unit(u0 + 2 * NF + j, it, 12)
                    pe.wait_ge(unit_lo_made, un.n + 1)
                    if m == 0 and p == 0:
                        pe.wait_ge(hid_done, f0 + NF - 1)
                    if m == 0 and p == 2:
                        pe.wait_ge(hid_done, f0 + NF)
                    if p == 0:
                        pe.wait_ge(x_ready, KD * (n + 1) + 4 * it + m - 3)
                    k0 = sum(DOWN[:p])
                    for k in range(DOWN[p]):
                        mm = product(m, *w_unit(un, k), g_hi, g_lo, k0 + k, k0 + k == 0, k0 + k == NF - 1)
                    mm.then_inc(unit_used, 1)

        def ffn_act(act, i, u0):
            n, f0 = FFN_NORM[i], NF * FFN_AT[i]

            def gate_up(it):
                for j in range(2):
                    t = f0 + 2 * it + j
                    split_hi(act, Unit(u0 + 2 * j + 2, it, 4))
                    if isinstance(it, int) and it == 0 and j == 0:
                        norm_act(act, n)
                    act.wait_ge(gate_scaled, t + 1)
                    nc.scalar.activation(silu_t[:], gate_t[:], ACT.Silu).then_inc(silu_made, 1)
                    split_hi(act, Unit(u0 + 2 * j + 3, it, 4))
                    act.wait_ge(hid_made, t + 1)
                    nc.scalar.copy(cols(g_hi, (2 * it + j) * T, T), hid_t[:]).then_inc(hid_hi_made, 1)

            gate_up(0)
            with act.Fori(1, NF // 2) as it:
                gate_up(it)

            def down(it):
                for j in range(12):
                    un = Unit(u0 + 2 * NF + j + 2, it, 12)
                    if not (isinstance(un.n, int) and un.n >= LAST_UNIT):
                        split_hi(act, un, DOWN[(j + 2) % 3] * P)
                    if j % 3 == 2 and n + 1 < len(stages):
                        publish_act(act, n + 1, 4 * it + j // 3)
            if u0 + NU["ffn"] < LAST_UNIT:
                with act.Fori(0, 2) as it:
                    down(it)
            else:
                down(0)
                down(1)

        def ffn_dve(dve, i, u0):
            n, f0 = FFN_NORM[i], NF * FFN_AT[i]

            def gate_up(it):
                for j in range(2):
                    t = f0 + 2 * it + j
                    split_lo(dve, Unit(u0 + 2 * j + 2, it, 4))
                    if isinstance(it, int) and it == 0 and j == 0:
                        norm_dve(dve, n)
                        dve.wait_ge(inv_made, ROW_USE[n] + 1)
                    dve.wait_ge(unit_used, Unit(u0 + 2 * j, it, 4).n + 1)
                    nc.vector.tensor_tensor(two(gate_t[:]), slot(2 * j), two(inv[:]), ALU.mult).then_inc(gate_scaled, 1)
                    split_lo(dve, Unit(u0 + 2 * j + 3, it, 4))
                    dve.wait_ge(unit_used, Unit(u0 + 2 * j + 1, it, 4).n + 1)
                    nc.vector.tensor_tensor(two(up_t[:]), slot(2 * j + 1), two(inv[:]), ALU.mult).then_inc(up_scaled, 1)
                    dve.wait_ge(silu_made, t + 1)
                    dve.wait_ge(up_scaled, t + 1)
                    if not (isinstance(t, int) and t == 0):
                        dve.wait_ge(hid_done, t)
                    nc.vector.tensor_tensor(hid_t[:], up_t[:], silu_t[:], ALU.mult).then_inc(hid_made, 1)
                    dve.wait_ge(hid_hi_made, t + 1)
                    nc.vector.tensor_tensor(cols(g_lo, (2 * it + j) * T, T), hid_t[:],
                                            cols(g_hi, (2 * it + j) * T, T), ALU.subtract).then_inc(hid_done, 1)

            gate_up(0)
            with dve.Fori(1, NF // 2) as it:
                gate_up(it)

            def down(it):
                for j in range(12):
                    un = Unit(u0 + 2 * NF + j + 2, it, 12)
                    if not (isinstance(un.n, int) and un.n >= LAST_UNIT):
                        split_lo(dve, un, DOWN[(j + 2) % 3] * P)
                    if j % 3 == 2:
                        m = j // 3
                        k = 4 * it + m
                        dve.wait_ge(unit_used, Unit(u0 + 2 * NF + j, it, 12).n + 1)
                        xk = two(cols(xT, k * T, T))
                        nc.vector.scalar_tensor_tensor(out=xk, in0=slot(m), scalar=0.5, in1=xk,
                                                       op0=ALU.mult, op1=ALU.add).then_inc(x_ready, 1)
                        if n + 1 < len(stages):
                            publish_dve(dve, n + 1, k)
            if u0 + NU["ffn"] < LAST_UNIT:
                with dve.Fori(0, 2) as it:
                    down(it)
            else:
                down(0)
                down(1)

        def add_sp(sp, u0, w, it):
            w = w.rearrange("(k p) d -> p k d", p=P)
            for j in range(4):
                load_unit(sp, Unit(u0 + j, it, 4), w[:, :, bass.ds((4 * it + j) * P, P)], UC, KD)

        def add_pe(pe, u0, n, mh, ml, operand=None):
            with pe.Fori(0, 2) as it:
                for j in range(4):
                    un = Unit(u0 + j, it, 4)
                    pe.wait_ge(unit_lo_made, un.n + 1)
                    pe.wait_ge(x_ready, KD * n + 4 * it + j - 3)
                    for k in range(KD):
                        if operand is not None and j == 0 and k in (0, KD - 1):
                            pe.wait_ge(operand, KD - 1 if k == 0 else KD)
                        mm = product(j, *w_unit(un, k), mh, ml, k, k == 0, k == KD - 1)
                    mm.then_inc(unit_used, 1)

        def add_act(act, u0, n, publish=True):
            with act.Fori(0, 2) as it:
                for j in range(4):
                    split_hi(act, Unit(u0 + j + 2, it, 4))
                    if publish:
                        publish_act(act, n, 4 * it + j)
            if not publish:
                with act.Fori(0, KD) as k:
                    publish_act(act, n, k)

        def add_dve(dve, u0, n, publish=True):
            with dve.Fori(0, 2) as it:
                for j in range(4):
                    split_lo(dve, Unit(u0 + j + 2, it, 4))
                    dve.wait_ge(unit_used, Unit(u0 + j, it, 4).n + 1)
                    xk = two(cols(xT, (4 * it + j) * T, T))
                    nc.vector.tensor_tensor(xk, slot(j), xk, ALU.add).then_inc(x_ready, 1)
                    if publish:
                        publish_dve(dve, n, 4 * it + j)
            if not publish:
                with dve.Fori(0, KD) as k:
                    publish_dve(dve, n, k)

        conv_u = a["w_conv_in"].rearrange("(k p) d -> p k d", p=P)

        def conv_sp(sp, u0):
            sp.dma_start(st_nat[:], a["state_conv"].rearrange("b j d -> (b j) d")).then_inc(state_in, 16)
            sp.dma_start(out["conv_sample"][:, 0, :], a["state_conv"][:, 1, :]).then_inc(stores, 16)
            with sp.Fori(0, 2) as it:
                for j in range(12):
                    part, m = j % 3, j // 3
                    load_unit(sp, Unit(u0 + j, it, 12), conv_u[:, :, bass.ds((4 * it + m + part * KD) * P, P)], UC, KD)
            with sp.Fori(0, 2) as it:
                add_sp(sp, u0 + 3 * KD, a["w_conv_out"], it)

        def conv_pe(pe, u0):
            n = CONV_NORM
            pe.wait_ge(state_in, 16)
            pe.wait_ge(x_ready, KD * n + 8)
            for m in range(KD):
                mm = nc.tensor.transpose(ps[:, 5, m * 2 * DEC:(m + 1) * 2 * DEC], st_nat[:, m * P:(m + 1) * P],
                                         ident[0:2 * DEC, 0:2 * DEC])
            mm.then_inc(state_T, 1)
            for j in range(3 * KD):
                un = Unit(u0 + j)
                pe.wait_ge(unit_lo_made, un.n + 1)
                if j == 2:
                    pe.wait_ge(state_copied, 1)
                if j == 3:
                    pe.wait_ge(inv_made, ROW_USE[n] + 1)
                if j >= 4:
                    pe.wait_ge(conv_read, (j - 4) // 3 + 1)
                for k in range(KD):
                    if j == 0:
                        pe.wait_ge(h_ready, KD * n + k + 1)
                    mm = product(j % 4, *w_unit(un, k), h_hi, h_lo, k, k == 0, k == KD - 1)
                mm.then_inc(unit_used, 1)
                if j == 0:
                    norm_pe(pe, n)
            pe.wait_ge(conv_read, KD)
            add_pe(pe, u0 + 3 * KD, n + 1, z_hi, z_lo, z_ready)
            pe.wait_ge(tail_made, 2 * KD)
            pe.wait_ge(x_ready, KD * (n + 1) + 5)
            for m in range(KD):
                mm = nc.tensor.transpose(ps[0:2 + DEC, m // 4, (m % 4) * P:(m % 4 + 1) * P], tail[:, m, :], ident[:])
            mm.then_inc(tail_T, 1)
            for b in range(2):
                pe.wait_ge(tails_copied[b], 1)

        def conv_act(act, u0):
            n = CONV_NORM

            def finish_tile(m):
                act.wait_ge(u_made, m + 1)
                nc.scalar.copy(tail[:, m, 0:2], ue[:, m % 2, DEC + SEQ:]).then_inc(tail_made, 1)
                nc.scalar.copy(tail[:, m, 2:], ue[:, m % 2, 0:DEC]).then_inc(tail_made, 1)
                act.wait_ge(z_made, m + 1)
                nc.scalar.copy(z_hi[:, m * T:(m + 1) * T], cz[:]).then_inc(zh_made, 1)

            for j in range(3 * KD):
                split_hi(act, Unit(u0 + j + 2))
                if j == 0:
                    norm_act(act, n)
                if j % 3 == 0 and j:
                    finish_tile(j // 3 - 1)
            finish_tile(KD - 1)
            add_act(act, u0 + 3 * KD, n + 1)
            act.wait_ge(tail_T, 1)
            nc.scalar.copy(tail_nat[:, 0:512], ps[0:2 + DEC, 0, :]).then_inc(tails_copied[0], 1)
            for b in range(2):
                act.wait_ge(tails_copied[b], 1)
            act.dma_start(out["conv_prompt"][0], tail_nat[0:2, :]).then_inc(stores, 16)
            act.dma_start(out["conv_sample"][:, 1, :], tail_nat[2:2 + DEC, :]).then_inc(stores, 16)

        def conv_dve(dve, u0, step):
            n = CONV_NORM
            step.link(nc.vector.memset(ue[:, :, DEC:DEC + 2], 0.0))
            dve.wait_ge(state_T, 1)
            nc.vector.tensor_copy(stT[:], ps[:, 5, 0:KD * 2 * DEC].rearrange("p (k r) -> p k r", k=KD)).then_inc(state_copied, 1)
            dve.wait_ge(state_copied, 1)

            def finish_tile(m):
                dve.wait_ge(zh_made, m + 1)
                nc.vector.tensor_tensor(z_lo[:, m * T:(m + 1) * T], cz[:], z_hi[:, m * T:(m + 1) * T],
                                        ALU.subtract).then_inc(z_ready, 1)
                dve.wait_ge(z_ready, m + 1)

            for j in range(3 * KD):
                split_lo(dve, Unit(u0 + j + 2))
                if j == 0:
                    norm_dve(dve, n)
                    dve.wait_ge(inv_made, ROW_USE[n] + 1)
                if j % 3 == 0 and j:
                    finish_tile(j // 3 - 1)
                if j % 3 != 2:
                    continue
                m = j // 3
                gb, gc, xv = (slot((j - 2 + q) % 4) for q in range(3))
                w = [gain[:, 6 * KD + q * KD + m:6 * KD + q * KD + m + 1] for q in range(CONV)]
                us = ue[:, m % 2, :]
                dve.wait_ge(unit_used, u0 + j + 1)
                step.link(nc.vector.tensor_tensor(two(ca[:]), gc, two(inv[:]), ALU.mult))
                step.link(nc.vector.tensor_tensor(two(cb[:]), xv, two(ca[:]), ALU.mult))
                nc.vector.tensor_tensor(two(cg[:]), gb, two(inv[:]), ALU.mult).then_inc(conv_read, 1)
                if m >= 2:
                    dve.wait_ge(tail_made, 2 * (m - 1))
                step.link(nc.vector.tensor_tensor(us[:, 0:DEC], cb[:, 0:DEC], inv[:, 0:DEC], ALU.mult))
                nc.vector.tensor_tensor(us[:, DEC + 2:], cb[:, DEC:], inv[:, DEC:], ALU.mult).then_inc(u_made, 1)
                dve.wait_ge(u_made, m + 1)
                past = stT[:, m, :].rearrange("p (b j) -> p j b", j=2)
                step.link(nc.vector.tensor_scalar(cy[:, 0:DEC], past[:, 0, :], w[0], None, ALU.mult))
                step.link(nc.vector.tensor_scalar(cy[:, DEC:], us[:, DEC:DEC + SEQ], w[0], None, ALU.mult))
                step.link(nc.vector.scalar_tensor_tensor(out=cy[:, 0:DEC], in0=past[:, 1, :], scalar=w[1],
                                                         in1=cy[:, 0:DEC], op0=ALU.mult, op1=ALU.add))
                step.link(nc.vector.scalar_tensor_tensor(out=cy[:, DEC:], in0=us[:, DEC + 1:DEC + 1 + SEQ], scalar=w[1],
                                                         in1=cy[:, DEC:], op0=ALU.mult, op1=ALU.add))
                step.link(nc.vector.scalar_tensor_tensor(out=cy[:, 0:DEC], in0=us[:, 0:DEC], scalar=w[2],
                                                         in1=cy[:, 0:DEC], op0=ALU.mult, op1=ALU.add))
                step.link(nc.vector.scalar_tensor_tensor(out=cy[:, DEC:], in0=us[:, DEC + 2:], scalar=w[2],
                                                         in1=cy[:, DEC:], op0=ALU.mult, op1=ALU.add))
                dve.wait_ge(conv_read, m + 1)
                nc.vector.tensor_tensor(cz[:], cy[:], cg[:], ALU.mult).then_inc(z_made, 1)
            finish_tile(KD - 1)
            add_dve(dve, u0 + 3 * KD, n + 1)
            dve.wait_ge(tail_T, 1)
            nc.vector.tensor_copy(tail_nat[:, 512:], ps[0:2 + DEC, 1, :]).then_inc(tails_copied[1], 1)

        KV_BANK = (5, 6, 0, 1, 2)
        TURN_BANK = (3, 4, 7)
        ORDER = (QT,) + tuple(range(QT))
        CQ, KV, UQ, UK, UV, WO = 0, 4, 8, 14, 16, 18
        J_K = 3 * NT
        J_Q = J_K + 2 * NT
        J_V = J_Q + 2
        J_QT = J_V + 2 * QT
        J_KT = J_QT + 3 * QT
        J_END = J_KT + 3 * QT
        rx, rcq, rlat, krss = 2, 5, 8, 9
        wuk_src = a["w_uk"].rearrange("(c p) h d -> p c (h d)", p=P)
        wuv_src = a["w_uv"].rearrange("(c p) h d -> p c (h d)", p=P)
        hv_hi = h_hi[:].rearrange("p (k t) -> p k t", k=KD)
        hv_lo = h_lo[:].rearrange("p (k t) -> p k t", k=KD)

        def turned_jobs(job):
            return 2 + job - J_QT + 1

        def mla_sp(sp, u0):
            n = MLA_NORM
            dq, dkv = (a[w].rearrange("(k p) c -> p k c", p=P) for w in ("w_dq", "w_dkv"))
            uq = a["w_uq"].rearrange("(k p) h d -> p k (h d)", p=P)
            for j in range(4):
                load_unit(sp, Unit(u0 + CQ + j), dq[:, 2 * j:2 * j + 2, :], UC, 2)
            sp.wait_ge(x_ready, KD * (n + 1))
            for dst, src in ((q_row, a["q_a_norm"]), (kv_row, a["kv_a_norm"]), (gk_row, a["k_norm"]), (gqk, a["q_norm"])):
                sp.dma_start(dst[:] if dst is not gqk else gqk, src.partition_broadcast(P)).then_inc(rows_in, 16)
            sp.dma_start(cosr[:], a["rope_cos"]).then_inc(rows_in, 16)
            sp.dma_start(sinr[:], a["rope_sin"]).then_inc(rows_in, 16)
            for j in range(4):
                load_unit(sp, Unit(u0 + KV + j), dkv[:, 2 * j:2 * j + 2, :], 2 * (CL + ROPE), 2)
            sp.dma_start(wu_raw[:], wuk_src).then_inc(wu_in, 16)
            for j in range(6):
                g, k = j // 2, 2 * (j % 2)
                load_unit(sp, Unit(u0 + UQ + j), uq[:, k:k + 2, g * 512:(g + 1) * 512], UC, 2)
            for g in range(2):
                load_unit(sp, Unit(u0 + UK + g), wuk_src[:, :, g * 512:(g + 1) * 512], UC, KC)
            for g in range(2):
                load_unit(sp, Unit(u0 + UV + g), wuv_src[:, :, g * 512:(g + 1) * 512], UC, KC)
            sp.wait_ge(latn_made, NT)
            sp.dma_start(out["latent_prompt"].rearrange("b (t p) c -> p (b t) c", p=P), lat[:, 0:QT, :]).then_inc(rows_out, 16)
            sp.dma_start(out["latent_sample"].rearrange("b o c -> (b o) c"), lat[0:DEC, QT, :]).then_inc(rows_out, 16)
            sp.wait_ge(kr_made, 1)
            sp.dma_start(out["krope_prompt"].rearrange("b (t p) c -> p (b t) c", p=P), kr[:, 0:QT, :]).then_inc(rows_out, 16)
            sp.dma_start(out["krope_sample"].rearrange("b o c -> (b o) c"), kr[0:DEC, QT, :]).then_inc(rows_out, 16)

            def sequence(b, s, used=None):
                cache = (cache0, cache1)[s]
                for p in range(PAGES):
                    row = a["page_table"][b:b + 1, p:p + 1] if isinstance(b, int) else a["page_table"][bass.ds(b, 1), p:p + 1]
                    page = sp.value_load(row, min_val=0, max_val=POOL - 1)
                    if p == 0 and used is not None:
                        sp.wait_ge(pv_made, used)
                        sp.wait_ge(cache_ones[s], 1)
                    sp.dma_start(cache[:, p, 0:CL], a["cache_latent"][bass.ds(page, 1)].rearrange("o p c -> p (o c)")
                                 ).then_inc(cache_in[s][p // 4], 16)
                    sp.dma_start(cache[:, p, KR:], a["cache_krope"][bass.ds(page, 1)].rearrange("o p c -> p (o c)")
                                 ).then_inc(cache_in[s][p // 4], 16)

            wo = a["w_o_attn"].rearrange("h v d -> (h v) d")
            add_sp(sp, u0 + WO, wo, 0)
            sp.wait_ge(s_new_read, 1)
            sequence(0, 0)
            sp.wait_ge(attn_left, 1)
            sequence(1, 1)
            sp.dma_start(wuv_raw[:], wuv_src).then_inc(wuv_in, 16)
            with sp.Fori(1, DEC // 2) as it:
                for s in range(2):
                    sequence(2 * it + s, s, 2 * it + s - 1)
            add_sp(sp, u0 + WO, wo, 1)

        def rows_product(dst, hi, lo, wh, wl, start, stop):
            nc.tensor.matmul(dst, hi, wh, start=start, stop=False)
            nc.tensor.matmul(dst, hi, wl, start=False, stop=False)
            return nc.tensor.matmul(dst, lo, wh, start=False, stop=stop)

        def mla_pe(pe, u0):
            n = MLA_NORM
            pe.wait_ge(x_ready, KD * n + 7)
            for u in range(4):
                un = Unit(u0 + CQ + u)
                pe.wait_ge(unit_lo_made, un.n + 1)
                pe.wait_ge(h_ready, KD * n + 2 * u + 2)
                for i in range(NT):
                    for kk in range(2):
                        k = 2 * u + kk
                        c0 = k * T + col0(i)
                        wh, wl = w_unit(un, kk, QR)
                        mm = rows_product(ps[:, i, :], h_hi[:, c0:c0 + P], h_lo[:, c0:c0 + P], wh, wl, k == 0, k == KD - 1)
                mm.then_inc(unit_used, 1)
                if u == 0:
                    pe.wait_ge(acc_done, KD * (n + 1))
                    for i in range(NT):
                        mm = nc.tensor.matmul(ps[:, 7, i:i + 1], acc[:, col0(i):col0(i) + P], ones[:, 0:1],
                                              start=True, stop=True)
                    mm.then_inc(stats_made, 1)
            for u in range(4):
                un = Unit(u0 + KV + u)
                pe.wait_ge(unit_lo_made, un.n + 1)
                for i in range(NT):
                    if u == 0 and i >= 2:
                        pe.wait_ge(cq_nat_made, i - 1)
                    for kk in range(2):
                        k = 2 * u + kk
                        c0 = k * T + col0(i)
                        wh, wl = w_unit(un, kk, CL + ROPE)
                        mm = rows_product(ps[:, KV_BANK[i], 0:CL + ROPE], h_hi[:, c0:c0 + P], h_lo[:, c0:c0 + P],
                                          wh, wl, k == 0, k == KD - 1)
                mm.then_inc(unit_used, 1)
            pe.wait_ge(cq_nat_made, NT)
            for t in range(2 * NT):
                i = t % NT
                pe.wait_ge(cqn_made if t < NT else latn_made, i + 1)
                if t >= 3:
                    pe.wait_ge(tv_lo_made, t - 2)
                for k in range(KQ if t < NT else KC):
                    src = cq_nat if t < NT else lat
                    mm = nc.tensor.transpose(ps[:, TURN_BANK[t % 3], k * P:(k + 1) * P], src[:, i, k * P:(k + 1) * P], ident[:])
                mm.then_inc(tv_made, 1)
            pe.wait_ge(tv_lo_made, 2 * NT)
            for j in range(6):
                un = Unit(u0 + UQ + j)
                pe.wait_ge(unit_lo_made, un.n + 1)
                for i in range(NT):
                    job = NT * (j // 2) + i
                    if j % 2 == 0 and job >= 8:
                        pe.wait_ge(job_read, job - 7)
                    for kk in range(2):
                        k = 2 * (j % 2) + kk
                        wh, wl = w_unit(un, kk, 512)
                        mm = rows_product(ps[:, job % 8, :], cq_hi[:, k, col0(i):col0(i) + P],
                                          cq_lo[:, k, col0(i):col0(i) + P], wh, wl, k == 0, k == KQ - 1)
                mm.then_inc(unit_used, 1)
            for g in range(2):
                pe.wait_ge(unit_lo_made, u0 + UK + g + 1)
                for i in range(NT):
                    job = J_K + NT * g + i
                    pe.wait_ge(job_read, job - 7)
                    for c in range(KC):
                        mm = rows_product(ps[:, job % 8, :], lt_hi[:, c, col0(i):col0(i) + P],
                                          lt_lo[:, c, col0(i):col0(i) + P], wuk_hi[:, c, g * 512:(g + 1) * 512],
                                          wuk_lo[:, c, g * 512:(g + 1) * 512], c == 0, c == KC - 1)
                mm.then_inc(unit_used, 1)
            pe.wait_ge(q_post_made, 1)
            for part in range(2):
                job = J_Q + part
                pe.wait_ge(job_read, job - 7)
                for h in range(H):
                    if part == 0:
                        mm = nc.tensor.transpose(ps[:, job % 8, h * DEC:(h + 1) * DEC],
                                                 q_nat[0:DEC, QT, h * HD:h * HD + NOPE], ident[0:DEC, 0:DEC])
                    else:
                        mm = nc.tensor.transpose(ps[0:ROPE, job % 8, h * DEC:(h + 1) * DEC],
                                                 q_rope[0:DEC, 0, h * ROPE:(h + 1) * ROPE], ident[0:DEC, 0:DEC])
                mm.then_inc(turned, 1)
            for g in range(2):
                un = Unit(u0 + UV + g)
                pe.wait_ge(unit_lo_made, un.n + 1)
                for i in range(QT):
                    job = J_V + QT * g + i
                    pe.wait_ge(job_read, job - 7)
                    for c in range(KC):
                        wh, wl = w_unit(un, c, 512)
                        mm = rows_product(ps[:, job % 8, :], lt_hi[:, c, col0(i):col0(i) + P],
                                          lt_lo[:, c, col0(i):col0(i) + P], wh, wl, c == 0, c == KC - 1)
                mm.then_inc(unit_used, 1)
            for i in range(QT):
                pe.wait_ge(q_post_made, i + 2)
                for part in range(3):
                    job = J_QT + 3 * i + part
                    pe.wait_ge(job_read, job - 7)
                    for e in range(4):
                        if part < 2:
                            src = q_nat[:, i, (4 * part + e) * HD:(4 * part + e) * HD + NOPE]
                        else:
                            src = q_rope[:, (i + 1) % 2, e * P:(e + 1) * P]
                        mm = nc.tensor.transpose(ps[:, job % 8, e * P:(e + 1) * P], src, ident[:])
                    mm.then_inc(turned, 1)
            for i in range(QT):
                pe.wait_ge(k_post_made, i + 1)
                for part in range(3):
                    job = J_KT + 3 * i + part
                    pe.wait_ge(job_read, job - 7)
                    for e in range(4):
                        if part < 2:
                            src = k_nat[:, i, (4 * part + e) * NOPE:(4 * part + e + 1) * NOPE]
                        else:
                            src = k_rope[:, i % 2, e * P:(e + 1) * P]
                        mm = nc.tensor.transpose(ps[:, job % 8, e * P:(e + 1) * P], src, ident[:])
                    mm.then_inc(turned, 1)
            absorb_pe(pe)
            prompt_pe(pe)
            decode_pe(pe)
            pe.wait_ge(os_lo_made, 1)
            add_pe(pe, u0 + WO, n + 1, h_hi, h_lo)

        def absorb_pe(pe):
            pe.wait_ge(job_read, J_END)
            pe.wait_ge(wu_in, 16)

            def turn(h):
                if h >= 2:
                    pe.wait_ge(wukT_made, h - 1)
                for c in range(KC):
                    mm = nc.tensor.transpose(ps[:, 1 + h % 2, c * P:(c + 1) * P], wu_raw[:, c, h * NOPE:(h + 1) * NOPE], ident[:])
                mm.then_inc(wuk_turned, 1)

            turn(0)
            for h in range(H):
                if h + 1 < H:
                    turn(h + 1)
                pe.wait_ge(wukT_made, h + 1)
                for c in range(KC):
                    o = c * H * DEC + h * DEC
                    mm = nc.tensor.matmul(ps[:, 0, o:o + DEC], wukT[:, h % 2, c * P:(c + 1) * P], qsT[:, h, :],
                                          start=True, stop=True)
                mm.then_inc(qa_heads, 1)
            nc.tensor.transpose(ps[0:ROPE, 4, 0:DEC], kr[0:DEC, QT, :], ident[0:DEC, 0:DEC]).then_inc(kr_turned, 1)
            pe.wait_ge(qa_made, 1)
            pe.wait_ge(kr_newT_made, 1)
            for c in range(KC):
                mm = rows_product(ps[:, 3, 0:DEC * H], lt_hi[:, c, 0:P], lt_lo[:, c, 0:P], qa_hi[:, c].rearrange("p b h -> p (b h)"),
                                  qa_lo[:, c].rearrange("p b h -> p (b h)"), c == 0, c == KC - 1)
                if c == 0:
                    nc.tensor.matmul(ps[0:DEC, 3, 0:DEC * H], kr_newT[:], qrT[:].rearrange("p b h -> p (b h)"),
                                     start=False, stop=False)
            mm.then_inc(s_new_raw, 1)

        def absorb_act(act):
            for h in range(H):
                act.wait_ge(wuk_turned, h + 1)
                if h >= 2:
                    act.wait_ge(qa_heads, h - 1)
                nc.scalar.copy(wukT[:, h % 2, :], ps[:, 1 + h % 2, 0:CL]).then_inc(wukT_made, 1)
            act.wait_ge(kr_turned, 1)
            nc.scalar.copy(kr_newT[:], ps[0:ROPE, 4, 0:DEC]).then_inc(kr_newT_made, 1)
            act.wait_ge(qa_heads, H)
            for c in range(KC):
                src = ps[:, 0, c * H * DEC:(c + 1) * H * DEC].rearrange("p (h b) -> p h b", h=H)
                nc.scalar.copy(qa_hi[:, c].rearrange("p b h -> p h b"), src).then_inc(qa_hi_made, 1)

        def absorb_dve(dve, step):
            dve.wait_ge(qa_hi_made, KC)
            for c in range(KC):
                src = ps[:, 0, c * H * DEC:(c + 1) * H * DEC].rearrange("p (h b) -> p h b", h=H)
                ins = nc.vector.tensor_tensor(qa_lo[:, c].rearrange("p b h -> p h b"), src,
                                              qa_hi[:, c].rearrange("p b h -> p h b"), ALU.subtract)
            ins.then_inc(qa_made, 1)
            dve.wait_ge(qa_made, 1)
            dve.wait_ge(s_new_raw, 1)
            step.link(nc.vector.tensor_tensor(s_new[:], ps[0:DEC, 3, 0:DEC * H].rearrange("p (b h) -> p b h", b=DEC),
                                              rk[0:DEC, QT, :].unsqueeze(1).to_broadcast([DEC, DEC, H]), ALU.mult))
            nc.vector.tensor_tensor(s_new[:], s_new[:], own[:], ALU.add).then_inc(s_new_read, 1)
            nc.vector.memset(cache0[:, :, ONE:ONE + 2], 1.0).then_inc(cache_ones[0], 1)

        def prompt_pe(pe):
            def values(h):
                pe.wait_ge(pt_made, 4 * h + 4)
                if h >= 2:
                    pe.wait_ge(o_lo_made, h - 1)
                for i in range(QT):
                    for j in range(i + 1):
                        mm = nc.tensor.matmul(ps[:, 6 + h % 2, i * P:(i + 1) * P], v[:, j, h * VD:(h + 1) * VD],
                                              pt[:, j, i * P:(i + 1) * P], start=(j == 0), stop=(j == i))
                mm.then_inc(o_made, 1)

            def turn(s):
                i = s % QT
                pe.wait_ge(pn_made, s + 1)
                if s >= 2:
                    pe.wait_ge(pt_made, s - 1)
                for j in range(i + 1):
                    mm = nc.tensor.transpose(ps[:, 4 + s % 2, j * P:(j + 1) * P], pn[:, s % 2, j * P:(j + 1) * P], ident[:])
                mm.then_inc(p_turned, 1)

            pe.wait_ge(s_new_read, 1)
            for s in range(QT * H + 3):
                if s < QT * H:
                    h, i = s // QT, s % QT
                    r = ROPE * (h % 2)
                    nk = (i + 1) * P
                    if s >= 4:
                        pe.wait_ge(exp_made, s - 3)
                    nc.tensor.matmul(ps[:, i, 0:nk], q_n[:, h, i * P:(i + 1) * P], k_n[:, h, 0:nk], start=True, stop=False)
                    nc.tensor.matmul(ps[:, i, 0:nk], q_r[r:r + ROPE, h // 2, i * P:(i + 1) * P], k_r[r:r + ROPE, h // 2, 0:nk],
                                     start=False, stop=True).then_inc(scores_made, 1)
                if s >= 6 and (s - 6) % 4 == 0:
                    values((s - 6) // 4)
                if 2 <= s < QT * H + 2:
                    turn(s - 2)

        def prompt_act(act):
            for s in range(QT * H + 3):
                if s < QT * H:
                    h, i = s // QT, s % QT
                    nk = (i + 1) * P
                    act.wait_ge(neg_made, s + 1)
                    if s >= 2:
                        act.wait_ge(p_turned, s - 1)
                    nc.scalar.activation(pn[:, s % 2, 0:nk], ps[:, i, 0:nk], ACT.Exp, bias=nb[:, s:s + 1],
                                         scale=qs[:, i, h:h + 1], accum_out=sums[:, s:s + 1]).then_inc(exp_made, 1)
                if 2 <= s < QT * H + 2:
                    e = s - 2
                    act.wait_ge(p_turned, e + 1)
                    if e % QT == 0 and e:
                        act.wait_ge(o_made, e // QT)
                    i = e % QT
                    nc.scalar.copy(pt[:, 0:i + 1, i * P:(i + 1) * P],
                                   ps[:, 4 + e % 2, 0:(i + 1) * P].rearrange("p (j q) -> p j q", j=i + 1)).then_inc(pt_made, 1)
                if s >= 7 and (s - 7) % 4 == 0:
                    head_hi(act, (s - 7) // 4)
            head_hi(act, H - 1)

        def head_hi(act, h):
            act.wait_ge(o_made, h + 1)
            nc.scalar.copy(hv_hi[:, h, DEC:], ps[:, 6 + h % 2, :]).then_inc(o_hi_made, 1)

        def head_lo(dve, h):
            dve.wait_ge(o_hi_made, h + 1)
            nc.vector.tensor_tensor(hv_lo[:, h, DEC:], ps[:, 6 + h % 2, :], hv_hi[:, h, DEC:], ALU.subtract).then_inc(o_lo_made, 1)

        def prompt_dve(dve, step):
            for s in range(QT * H + 1):
                if s < QT * H:
                    h, i = s // QT, s % QT
                    nk = (i + 1) * P
                    dve.wait_ge(scores_made, s + 1)
                    step.link(nc.vector.tensor_tensor(ps[:, i, i * P:nk], ps[:, i, i * P:nk], causal[:], ALU.add))
                    step.link(nc.vector.tensor_reduce(mxp[:, s:s + 1], ps[:, i, 0:nk], AX.X, ALU.max))
                    nc.vector.scalar_tensor_tensor(out=nb[:, s:s + 1], in0=mxp[:, s:s + 1], scalar=-1.0,
                                                   in1=qs[:, i, h:h + 1], op0=ALU.mult, op1=ALU.mult).then_inc(neg_made, 1)
                if s >= 1:
                    e = s - 1
                    nk = (e % QT + 1) * P
                    dve.wait_ge(exp_made, e + 1)
                    step.link(nc.vector.reciprocal(rs[:, e:e + 1], sums[:, e:e + 1]))
                    nc.vector.tensor_scalar(pn[:, e % 2, 0:nk], pn[:, e % 2, 0:nk], rs[:, e:e + 1], None,
                                            ALU.mult).then_inc(pn_made, 1)
                if s >= 8 and s % 4 == 0:
                    head_lo(dve, s // 4 - 2)
            head_lo(dve, H - 1)

        SPAN = ((0, 384), (384, 384), (768, 264))

        def decode_pe(pe):
            def turn(s, t, g, it):
                cache = (cache0, cache1)[s]
                if t % 4 == 0:
                    pe.wait_ge(cache_in[s][t // 4], 128 * (it + 1))
                if not (isinstance(g, int) and g < 2):
                    pe.wait_ge(latl_made, g - 1)
                    pe.wait_ge(krt_made, g - 1)
                o = 6 + t % 2
                for c in range(KC):
                    nc.tensor.transpose(ps[:, o, c * P:(c + 1) * P], cache[:, t, c * P:(c + 1) * P], ident[:])
                nc.tensor.transpose(ps[0:ROPE, o, CL:CL + P], cache[:, t, KR:KR + ROPE], ident[:]).then_inc(t_made, 1)

            def values(s, cnt, w):
                cache = (cache0, cache1)[s]
                o = 3 * (w % 2)
                pe.wait_ge(pr_made, cnt)
                for t in range(PAGES):
                    nc.tensor.matmul(ps[0:H, o, 0:CL + 1], pr[:, s, t, :], cache[:, t, 0:CL + 1], start=(t == 0), stop=False)
                nc.tensor.matmul(ps[0:H, o, 0:CL + 1], pr[0:DEC, s, PAGES, :], latnew[:], start=False,
                                 stop=True).then_inc(pv_made, 1)

            def turn_out(cnt, bank):
                pe.wait_ge(ident_made, 1)
                pe.wait_ge(ol_made, cnt)
                for c in range(KC):
                    mm = nc.tensor.transpose(ps[:, bank, CL + P + c * H:CL + P + (c + 1) * H], ol[:, c * P:(c + 1) * P],
                                             ident[0:H, 0:H])
                mm.then_inc(ol_turned, 1)

            def pair(it, last):
                first = isinstance(it, int) and it == 0
                for s in range(2):
                    for t in range(PAGES):
                        g = 2 * PAGES * it + PAGES * s + t
                        w = (PAGES + 1) * s + t + (t >= PAGES // 2)
                        prev = not (first and s == 0)
                        b = 2 * it + s
                        if t == PAGES // 2 and prev:
                            pe.wait_ge(squares_made, g - 1)
                            pe.wait_ge(scores_copied, g - 1)
                            values(1 - s, b, w - 1)
                        if t == 12 and prev:
                            pe.wait_ge(oT_made, b)
                        if not (last and s == 1 and t == PAGES - 1):
                            if t < PAGES - 1:
                                turn(s, t + 1, g + 1, it)
                            else:
                                turn_next(1 - s, g + 1, it if s == 0 else it + 1)
                        keys_at(s, t, g, w, b, prev)
                        if t == 11 and prev:
                            turn_out(b, 7)

            def turn_next(s, g, it):
                pe.wait_ge(cache_ones[s], 1)
                turn(s, 0, g, it)

            def keys_at(s, t, g, w, b, prev):
                first = isinstance(g, int) and g < 2
                o = 3 * (w % 2)
                pe.wait_ge(latl_made, g + 1)
                pe.wait_ge(krt_made, g + 1)
                if t == 0:
                    pe.wait_ge(query_set, b + 1)
                if not first:
                    for c in (squares_made, scores_copied):
                        pe.wait_ge(c, g if t == PAGES // 2 else g - 1)
                if t == PAGES // 2 + 1 and prev:
                    pe.wait_ge(ol_made, b)
                for c in range(KC):
                    th, tl = latT_hi[:, t % 2, c * P:(c + 1) * P], latT_lo[:, t % 2, c * P:(c + 1) * P]
                    for q, (x, wd) in enumerate(((th, wuk_hi), (th, wuk_lo), (tl, wuk_hi))):
                        for e, (c0, nn) in enumerate(SPAN):
                            mm = nc.tensor.matmul(ps[:, o + e, 0:nn], x, wd[:, c, c0:c0 + nn],
                                                  start=(c == 0 and q == 0), stop=(c == KC - 1 and q == 2))
                        if c == 0 and q == 0:
                            nc.tensor.matmul(ps[:, o + 2, 2 * P:2 * P + H], krT[:, t % 2, :], qrb[:], start=False, stop=False)
                mm.then_inc(k_made, 1)

            pe.wait_ge(o_lo_made, H)
            turn_next(0, 0, 0)
            pair(0, False)
            with pe.Fori(1, DEC // 2 - 1) as it:
                pair(it, False)
            pair(DEC // 2 - 1, True)
            for c in (squares_made, scores_copied):
                pe.wait_ge(c, DEC * PAGES)
            values(1, DEC, 0)
            turn_out(DEC, 7)
            pe.wait_ge(wuv_in, 16)
            pe.wait_ge(oT_made, DEC)
            for h in range(H):
                for c in range(KC):
                    mm = nc.tensor.matmul(ps[:, 3, h * DEC:(h + 1) * DEC], wuv_raw[:, c, h * VD:(h + 1) * VD], oT[:, c, h, :],
                                          start=(c == 0), stop=(c == KC - 1))
            mm.then_inc(os_made, 1)

        def decode_act(act):
            def latT(t, g):
                act.wait_ge(t_made, g + 1)
                if not (isinstance(g, int) and g < 2):
                    act.wait_ge(k_made, g - 1)
                o = 6 + t % 2
                nc.scalar.copy(krT[:, t % 2, :], ps[0:ROPE, o, CL:CL + P]).then_inc(krt_made, 1)
                nc.scalar.copy(latT_hi[:, t % 2, :], ps[:, o, 0:CL]).then_inc(lath_made, 1)

            def squares(t, g, w):
                o = 3 * (w % 2)
                act.wait_ge(k_made, g + 1)
                if not (isinstance(g, int) and g < 2):
                    act.wait_ge(kss_made, g - 1)
                for e, (c0, nn) in enumerate(SPAN):
                    nn = min(nn, H * NOPE - c0)
                    ins = nc.scalar.activation(ksq[:, t % 2, c0:c0 + nn], ps[:, o + e, 0:nn], ACT.Square)
                ins.then_inc(squares_made, 1)

            def softmax_part(s, cnt, t):
                cache = (cache0, cache1)[s]
                if t == 0:
                    if not (isinstance(cnt, int) and cnt < 2):
                        act.wait_ge(krs_made, cnt - 1)
                    nc.scalar.activation(krq[:], cache[:, :, KR:KR + ROPE], ACT.Square).then_inc(krq_made, 1)
                if t == 2:
                    act.wait_ge(kinv_made, cnt)
                    nc.scalar.activation(kroot[:], kinv[:], ACT.Sqrt).then_inc(kroot_made, 1)
                if t == 6:
                    act.wait_ge(sc_ready, cnt)
                    nc.scalar.activation(pr[:, s], sc[:, s], ACT.Exp).then_inc(pr_made, 1)

            def pair(it, last):
                first = isinstance(it, int) and it == 0
                for s in range(2):
                    for t in range(PAGES):
                        g = 2 * PAGES * it + PAGES * s + t
                        if not (last and s == 1 and t == PAGES - 1):
                            latT((t + 1) % PAGES, g + 1)
                        if not (first and s == 0):
                            softmax_part(1 - s, 2 * it + s, t)
                        squares(t, g, (PAGES + 1) * s + t + (t >= PAGES // 2))

            latT(0, 0)
            pair(0, False)
            with act.Fori(1, DEC // 2 - 1) as it:
                pair(it, False)
            pair(DEC // 2 - 1, True)
            for t in (0, 2, 6):
                softmax_part(1, DEC, t)
            act.wait_ge(os_made, 1)
            nc.scalar.copy(hv_hi[:, :, 0:DEC], ps[:, 3, 0:H * DEC].rearrange("p (h b) -> p h b", h=H)).then_inc(os_hi_made, 1)

        def decode_pool(pool):
            pool.wait_ge(mx_made, 1)
            nc.gpsimd.partition_all_reduce(mxa[:], mx8[:], P, bass.bass_isa.ReduceOp.max).then_inc(mxa_made, 1)
            pool.wait_ge(s_new_read, 1)
            with pool.Fori(2, DEC + 1) as count:
                pool.wait_ge(s_new_read, 1)
                pool.wait_ge(mx_made, count)
                nc.gpsimd.partition_all_reduce(mxa[:], mx8[:], P, bass.bass_isa.ReduceOp.max).then_inc(mxa_made, 1)

        def decode_dve(dve, step):
            step.link(nc.vector.memset(sc[:, :, PAGES, :], NEG))
            nc.vector.memset(cache1[:, :, ONE:ONE + 2], 1.0).then_inc(cache_ones[1], 1)

            def query(b):
                if not (isinstance(b, int) and b == 0):
                    dve.wait_ge(k_made, PAGES * b)
                one = (lambda t: t[:, :, b, :]) if isinstance(b, int) else (
                    lambda t: t[:, :, bass.ds(b, 1), :].rearrange("p c o h -> p c (o h)"))
                nc.vector.tensor_copy(wuk_hi[:, :, H * NOPE:], one(qa_hi))
                nc.vector.tensor_copy(wuk_lo[:, :, H * NOPE:], one(qa_lo))
                src = qrT[:, b, :] if isinstance(b, int) else qrT[:, bass.ds(b, 1), :].rearrange("p o h -> p (o h)")
                nc.vector.tensor_copy(qrb[:], src).then_inc(query_set, 1)

            def lo(t, g):
                dve.wait_ge(lath_made, g + 1)
                nc.vector.tensor_tensor(latT_lo[:, t % 2, :], ps[:, 6 + t % 2, 0:CL], latT_hi[:, t % 2, :],
                                        ALU.subtract).then_inc(latl_made, 1)

            def sums_of(s, t, g, w):
                o = 3 * (w % 2)
                dve.wait_ge(squares_made, g + 1)
                nc.vector.tensor_copy(sc[:, s, t, :], ps[:, o + 2, 2 * P:2 * P + H]).then_inc(scores_copied, 1)
                nc.vector.tensor_reduce(kss[:, s, t, :], ksq[:, t % 2, :].rearrange("p (h d) -> p h d", h=H), AX.X,
                                        ALU.add).then_inc(kss_made, 1)

            def softmax_part(s, cnt, t, g, o=0):
                if t == 0:
                    dve.wait_ge(krq_made, cnt)
                    nc.vector.tensor_reduce(krs[:], krq[:], AX.X, ALU.add).then_inc(krs_made, 1)
                if t == 1:
                    dve.wait_ge(krs_made, cnt)
                    dve.wait_ge(kss_made, g)
                    nc.vector.tensor_tensor(kms[:], kss[:, s], krs[:].unsqueeze(2).to_broadcast([P, PAGES, H]),
                                            ALU.add).then_inc(kms_made, 1)
                    dve.wait_ge(kms_made, 2 * cnt - 1)
                    nc.vector.tensor_scalar(kms[:], kms[:], 1.0 / HD, EPS, ALU.mult, ALU.add).then_inc(kms_made, 1)
                    dve.wait_ge(kms_made, 2 * cnt)
                    nc.vector.reciprocal(kinv[:], kms[:]).then_inc(kinv_made, 1)
                if t == 3:
                    dve.wait_ge(kroot_made, cnt)
                    dve.wait_ge(scores_copied, g)
                    nc.vector.tensor_tensor(sc[:, s, 0:PAGES, :], sc[:, s, 0:PAGES, :], kroot[:], ALU.mult).then_inc(sc_scaled, 1)
                    src = s_new[:, cnt - 1, :] if isinstance(cnt, int) else (
                        s_new[:, bass.ds(cnt - 1, 1), :].rearrange("p o h -> p (o h)"))
                    nc.vector.tensor_copy(sc[0:DEC, s, PAGES, :], src).then_inc(sc_scaled, 1)
                    dve.wait_ge(sc_scaled, 2 * cnt)
                    nc.vector.tensor_reduce(mx8[:], sc[:, s].rearrange("p t h -> p h t"), AX.X, ALU.max).then_inc(mx_made, 1)
                if t == 5:
                    dve.wait_ge(mxa_made, cnt)
                    nc.vector.tensor_tensor(sc[:, s], sc[:, s], mxa[:].unsqueeze(1).to_broadcast([P, PAGES + 1, H]),
                                            ALU.subtract).then_inc(sc_ready, 1)
                if t == 8:
                    dve.wait_ge(pv_made, cnt)
                    nc.vector.reciprocal(rden[:], ps[0:H, o, CL:CL + 1]).then_inc(rden_made, 1)
                    dve.wait_ge(rden_made, cnt)
                    nc.vector.tensor_scalar(ol[:], ps[0:H, o, 0:CL], rden[:], None, ALU.mult).then_inc(ol_made, 1)
                if t == 11:
                    dve.wait_ge(ol_turned, cnt)
                    src = ps[:, 7, CL + P:CL + P + KC * H].rearrange("p (c h) -> p c h", c=KC)
                    dst = (oT[:, :, :, cnt - 1] if isinstance(cnt, int)
                           else oT[:, :, :, bass.ds(cnt - 1, 1)].rearrange("p c h o -> p c (h o)"))
                    nc.vector.tensor_copy(dst, src).then_inc(oT_made, 1)

            def pair(it, last):
                first = isinstance(it, int) and it == 0
                for s in range(2):
                    b = 2 * it + s
                    for t in range(PAGES):
                        g = 2 * PAGES * it + PAGES * s + t
                        if not (last and s == 1 and t == PAGES - 1):
                            lo((t + 1) % PAGES, g + 1)
                        if not (first and s == 0):
                            softmax_part(1 - s, b, t, g, 3 * (((PAGES + 1) * s + PAGES // 2) % 2))
                        if t == PAGES - 1 and not (last and s == 1):
                            query(b + 1)
                        sums_of(s, t, g, (PAGES + 1) * s + t + (t >= PAGES // 2))

            lo(0, 0)
            query(0)
            pair(0, False)
            with dve.Fori(1, DEC // 2 - 1) as it:
                pair(it, False)
            pair(DEC // 2 - 1, True)
            for t in (0, 1, 3, 5, 8, 11):
                softmax_part(1, DEC, t, DEC * PAGES)
            dve.wait_ge(os_hi_made, 1)
            nc.vector.tensor_tensor(hv_lo[:, :, 0:DEC], ps[:, 3, 0:H * DEC].rearrange("p (h b) -> p h b", h=H),
                                    hv_hi[:, :, 0:DEC], ALU.subtract).then_inc(os_lo_made, 1)

        def mla_act(act, u0):
            n = MLA_NORM
            hi = lambda u, m_=UC, dst=None: split_hi(act, Unit(u0 + u), m_, dst)
            nkv = 2 * (CL + ROPE)

            def root(index, dst, src, scale=1.0):
                act.wait_ge(row_rec, index + 1)
                nc.scalar.activation(dst, src, ACT.Sqrt, scale=scale).then_inc(row_root, 1)

            def read_job(job, dst, src):
                nc.scalar.copy(dst, src).then_inc(job_read, 1)

            hi(2)
            root(0, st[:, rx, :], st[:, rx - 1, :])
            hi(3)
            hi(4, nkv)
            hi(5, nkv)
            act.wait_ge(unit_used, u0 + KV)
            act.wait_ge(row_root, 1)
            act.wait_ge(acc_done, KD * (n + 1))
            act.wait_ge(sq_made, KD * (n + 1))
            for i in range(NT):
                if i:
                    act.wait_ge(cq_nat_made, i)
                nc.scalar.activation(sq[:, 0:QR], ps[:, i, :], ACT.Square, scale=st[:, rx, i:i + 1], accum_out=st[:, 3, i:i + 1])
                nc.scalar.activation(cq_nat[:, i, :], ps[:, i, :], ACT.Copy, scale=st[:, rx, i:i + 1]).then_inc(cq_nat_made, 1)
            hi(6, nkv)
            root(1, st[:, rcq, :], st[:, rcq - 1, :])
            hi(7, nkv)
            hi(8)
            hi(9)
            act.wait_ge(cq_nat_made, NT)
            for i in range(NT):
                if i:
                    act.wait_ge(kv_nat_made, i)
                src = ps[:, KV_BANK[i], 0:CL + ROPE]
                nc.scalar.activation(sq[:, 0:CL], src[:, 0:CL], ACT.Square, scale=st[:, rx, i:i + 1], accum_out=st[:, 6, i:i + 1])
                nc.scalar.activation(kv_nat[:, i, :], src, ACT.Copy, scale=st[:, rx, i:i + 1]).then_inc(kv_nat_made, 1)
            for t in range(2 * NT):
                if t == NT:
                    root(2, st[:, rlat, :], st[:, rlat - 1, :])
                i = t % NT
                act.wait_ge(tv_made, t + 1)
                dst, kk = (cq_hi, KQ) if t < NT else (lt_hi, KC)
                src = ps[:, TURN_BANK[t % 3], 0:kk * P].rearrange("p (k q) -> p k q", k=kk)[:, :, 0:width(i)]
                nc.scalar.copy(dst[:, :, col0(i):col0(i) + width(i)], src).then_inc(tv_hi_made, 1)
            for g in range(3):
                hi(UQ + 2 * g + 2, UC, wuk_part(wuk_hi, 0) if g == 2 else None)
                hi(UQ + 2 * g + 3, UC, wuk_part(wuk_hi, 1) if g == 2 else None)
                act.wait_ge(unit_used, u0 + UQ + 2 * g + 2)
                for i in range(NT):
                    job = NT * g + i
                    read_job(job, q_nat[:, i, g * 512:(g + 1) * 512], ps[:, job % 8, :])

            def keys(g, i):
                job = J_K + NT * g + i
                for e in range(4):
                    if g or i or e:
                        act.wait_ge(ksum_made, 4 * (NT * g + i) + e)
                    nc.scalar.activation(sq[:, 0:NOPE], ps[:, job % 8, e * NOPE:(e + 1) * NOPE], ACT.Square,
                                         accum_out=rk[:, i, 4 * g + e:4 * g + e + 1]).then_inc(ksum_made, 1)
                if i < QT:
                    read_job(job, k_nat[:, i, g * 512:(g + 1) * 512], ps[:, job % 8, :])
                else:
                    act.wait_ge(ksum_made, 4 * (NT * g + i + 1))
                    nc.scalar.copy(sq[:, NOPE:NOPE + 1], ps[:, job % 8, 0:1]).then_inc(job_read, 1)

            def q_square(o):
                act.wait_ge(rope_made, o + 1)
                nc.scalar.activation(sqs[:], q_nat[:, ORDER[o], :], ACT.Square).then_inc(qsq_made, 1)
                root(3 + o, qs[:, ORDER[o], :], nb[:, H:2 * H], ATTN_SCALE ** 2)

            def read_q(o):
                if o == 0:
                    act.wait_ge(turned, 2)
                    read_job(J_Q, qsT[:], ps[:, J_Q % 8, 0:H * DEC].rearrange("p (h b) -> p h b", h=H))
                    read_job(J_Q + 1, qrT[:].rearrange("p b h -> p h b"),
                             ps[0:ROPE, (J_Q + 1) % 8, 0:H * DEC].rearrange("p (h b) -> p h b", h=H))
                    return
                read_turned(J_QT + 3 * (o - 1), o - 1, q_n, q_r)

            def read_turned(j0, i, dn, dr):
                for part in range(3):
                    act.wait_ge(turned, turned_jobs(j0 + part))
                    dst = dn[:, 4 * part:4 * part + 4, i * P:(i + 1) * P] if part < 2 else dr[:, :, i * P:(i + 1) * P]
                    read_job(j0 + part, dst, ps[:, (j0 + part) % 8, :].rearrange("p (e q) -> p e q", e=4))

            def values(g):
                hi(UV + g + 2)
                for i in range(QT):
                    job = J_V + QT * g + i
                    read_job(job, v[:, i, g * 512:(g + 1) * 512], ps[:, job % 8, :])

            hi(16)
            for i in range(NT):
                keys(0, i)
            q_square(0)
            hi(17)
            for i in range(NT):
                keys(1, i)
            read_q(0)
            q_square(1)
            values(0)
            q_square(2)
            values(1)
            q_square(3)
            act.wait_ge(rows_out, 16 * 4)
            read_q(1)
            q_square(4)
            read_q(2)
            act.wait_ge(q_post_made, NT)
            read_q(3)
            read_q(4)
            root(3 + NT, rk[:], stat8[:])
            for i in range(QT):
                read_turned(J_KT + 3 * i, i, k_n, k_r)
            absorb_act(act)
            prompt_act(act)
            decode_act(act)
            add_act(act, u0 + WO, n + 1, publish=False)

        def wuk_part(w, g):
            return w[:, :, g * 512:(g + 1) * 512]

        def mla_dve(dve, u0, step):
            n = MLA_NORM
            link = step.link

            def lo(u, m_=UC, dst=None):
                split_lo(dve, Unit(u0 + u), m_, dst)

            nkv = 2 * (CL + ROPE)

            def rec(index, dst, tmp, src, scale):
                link(nc.vector.tensor_scalar(tmp, src, scale, EPS, ALU.mult, ALU.add))
                nc.vector.reciprocal(dst, tmp).then_inc(row_rec, 1)
                dve.wait_ge(row_rec, index + 1)

            lo(2)
            dve.wait_ge(stats_made, n + 1)
            rec(0, st[:, rx - 1, :], st[:, rx - 2, :], ps[:, 7, 0:NT], 1.0 / D)
            nc.vector.memset(acc[:], 0.0).then_inc(acc_cleared, 1)
            lo(3)
            lo(4, nkv)
            lo(5, nkv)
            dve.wait_ge(cq_nat_made, NT)
            rec(1, st[:, rcq - 1, :], st[:, 10, :], st[:, 3, :], 1.0 / QR)
            lo(6, nkv)
            dve.wait_ge(rows_in, 16 * 6)
            dve.wait_ge(row_root, 2)
            link(nc.vector.tensor_tensor(gqk, gqk, gk_row[:], ALU.mult))
            for i in range(NT):
                nc.vector.scalar_tensor_tensor(out=cq_nat[:, i, :], in0=cq_nat[:, i, :], scalar=st[:, rcq, i:i + 1],
                                               in1=q_row[:], op0=ALU.mult, op1=ALU.mult).then_inc(cqn_made, 1)
            lo(7, nkv)
            lo(8)
            lo(9)
            dve.wait_ge(kv_nat_made, NT)
            rec(2, st[:, rlat - 1, :], st[:, 10, :], st[:, 6, :], 1.0 / CL)

            def turned_lo(t):
                i = t % NT
                dve.wait_ge(tv_hi_made, t + 1)
                dh, dl, kk = (cq_hi, cq_lo, KQ) if t < NT else (lt_hi, lt_lo, KC)
                c = slice(col0(i), col0(i) + width(i))
                src = ps[:, TURN_BANK[t % 3], 0:kk * P].rearrange("p (k q) -> p k q", k=kk)[:, :, 0:width(i)]
                nc.vector.tensor_tensor(dl[:, :, c], src, dh[:, :, c], ALU.subtract).then_inc(tv_lo_made, 1)

            for t in range(NT):
                turned_lo(t)
            dve.wait_ge(row_root, 3)
            for i in range(NT):
                nc.vector.scalar_tensor_tensor(out=lat[:, i, :], in0=kv_nat[:, i, 0:CL], scalar=st[:, rlat, i:i + 1],
                                               in1=kv_row[:], op0=ALU.mult, op1=ALU.mult).then_inc(latn_made, 1)
            for t in range(NT, 2 * NT):
                turned_lo(t)

            def rotate(x1, x2, o1, o2, cos, sin, t):
                link(nc.vector.tensor_tensor(t[0], x1, cos, ALU.mult))
                link(nc.vector.tensor_tensor(t[1], x2, sin, ALU.mult))
                link(nc.vector.tensor_tensor(t[2], x1, sin, ALU.mult))
                link(nc.vector.tensor_tensor(t[3], x2, cos, ALU.mult))
                link(nc.vector.tensor_tensor(o1, t[0], t[1], ALU.subtract))
                return nc.vector.tensor_tensor(o2, t[2], t[3], ALU.add)

            rotate(kv_nat[:, :, CL:CL + RH], kv_nat[:, :, CL + RH:], kr[:, :, 0:RH], kr[:, :, RH:], cosr[:], sinr[:],
                   [kt[:, q] for q in range(4)]).then_inc(kr_made, 1)
            dve.wait_ge(kr_made, 1)
            ktf = kt[:].rearrange("p a t c -> p (a t c)")[:, 0:NT * ROPE].rearrange("p (t c) -> p t c", t=NT)
            link(nc.vector.tensor_tensor(ktf, kr, kr, ALU.mult))
            link(nc.vector.tensor_reduce(st[:, krss, :], ktf, AX.X, ALU.add))
            dve.wait_ge(latn_made, NT)
            nc.vector.tensor_copy(latnew[:, 0:CL], lat[0:DEC, QT, :]).then_inc(latnew_made, 1)
            for u in range(10, 16):
                lo(u, UC, (wuk_part(wuk_hi, u - 14), wuk_part(wuk_lo, u - 14)) if u >= 14 else None)

            def q_rotate(o):
                i = ORDER[o]
                x = q_nat[:, i, :].rearrange("p (h d) -> p h d", h=H)
                t = sqs[:, 0:4 * H * RH].rearrange("p (a h c) -> p a h c", a=4, h=H)
                bc = lambda w: w[:, i, :].unsqueeze(1).to_broadcast([P, H, RH])
                rotate(x[:, :, NOPE:NOPE + RH], x[:, :, NOPE + RH:], x[:, :, NOPE:NOPE + RH], x[:, :, NOPE + RH:],
                       bc(cosr), bc(sinr), [t[:, q] for q in range(4)]).then_inc(rope_made, 1)

            def q_norm(o):
                i = ORDER[o]
                x = q_nat[:, i, :].rearrange("p (h d) -> p h d", h=H)
                qr = q_rope[:, o % 2, :].rearrange("p (h d) -> p h d", h=H)
                if o >= 1:
                    dve.wait_ge(row_root, 3 + o)
                dve.wait_ge(qsq_made, o + 1)
                link(nc.vector.tensor_reduce(mxp[:, 0:H], sqs[:].rearrange("p (h d) -> p h d", h=H), AX.X, ALU.add))
                rec(3 + o, nb[:, H:2 * H], nb[:, 0:H], mxp[:, 0:H], 1.0 / HD)
                if o >= 2:
                    dve.wait_ge(turned, 2 + 3 * (o - 2))
                link(nc.vector.tensor_tensor(x[:, :, 0:NOPE], x[:, :, 0:NOPE],
                                             gqk[:, 0:NOPE].unsqueeze(1).to_broadcast([P, H, NOPE]), ALU.mult))
                ins = nc.vector.tensor_tensor(qr, x[:, :, NOPE:], gqk[:, NOPE:].unsqueeze(1).to_broadcast([P, H, ROPE]), ALU.mult)
                if o == 0:
                    link(ins)
                    dve.wait_ge(row_root, 4)
                    xs, qrs = x[0:DEC], qr[0:DEC]
                    link(nc.vector.tensor_tensor(xs[:, :, 0:NOPE], xs[:, :, 0:NOPE],
                                                 qs[0:DEC, QT, :].unsqueeze(2).to_broadcast([DEC, H, NOPE]), ALU.mult))
                    ins = nc.vector.tensor_tensor(qrs, qrs, qs[0:DEC, QT, :].unsqueeze(2).to_broadcast([DEC, H, ROPE]), ALU.mult)
                ins.then_inc(q_post_made, 1)

            dve.wait_ge(job_read, J_K)
            q_rotate(0)
            lo(16)
            q_norm(0)
            lo(17)
            for o in range(1, NT):
                q_rotate(o)
                q_norm(o)
            dve.wait_ge(job_read, J_Q)
            link(nc.vector.tensor_tensor(stat8[:], rk[:], st[:, krss, :].unsqueeze(2).to_broadcast([P, NT, H]), ALU.add))
            rec(3 + NT, stat8[:], stat8[:], stat8[:], 1.0 / HD)
            dve.wait_ge(row_root, 4 + NT)
            for i in range(QT):
                x = k_nat[:, i, :].rearrange("p (h d) -> p h d", h=H)
                link(nc.vector.tensor_tensor(x, x, rk[:, i, :].unsqueeze(2).to_broadcast([P, H, NOPE]), ALU.mult))
                if i >= 2:
                    dve.wait_ge(turned, turned_jobs(J_KT + 3 * (i - 2) + 2))
                nc.vector.tensor_tensor(k_rope[:, i % 2, :].rearrange("p (h d) -> p h d", h=H),
                                        kr[:, i, :].unsqueeze(1).to_broadcast([P, H, ROPE]),
                                        rk[:, i, :].unsqueeze(2).to_broadcast([P, H, ROPE]), ALU.mult).then_inc(k_post_made, 1)
            lo(18)
            lo(19)
            absorb_dve(dve, step)
            prompt_dve(dve, step)
            dve.wait_ge(o_lo_made, H)
            nc.vector.memset(rden[:], 0.0).then_inc(attn_left, 1)
            dve.wait_ge(attn_left, 1)
            decode_dve(dve, step)
            add_dve(dve, u0 + WO, n + 1, publish=False)

        def start_sp(sp):
            rows = [a["norm_ffn1"][0], a["norm_mix"][0], a["norm_ffn2"][0],
                    a["norm_ffn1"][1], a["norm_mix"][1], a["norm_ffn2"][1]] + [a["conv_w"][j] for j in range(CONV)]
            for t in range(QT):
                sp.dma_start(x_nat[:, t, :], a["x_prompt"][0, t * P:(t + 1) * P, :]).then_inc(x_in, 16)
            sp.dma_start(xs_nat[:], a["x_sample"].rearrange("b o d -> (b o) d")).then_inc(x_in, 16)
            for n, r in enumerate(rows):
                sp.dma_start(gain_rows[KD * n:KD * (n + 1), :], r.rearrange("(k p) -> k p", p=P)).then_inc(x_in, 16)

        def start_pool(pool):
            step = Chain(pool, pool_step)
            step.link(nc.gpsimd.memset(ident[:], 0.0))
            nc.gpsimd.affine_select(out=ident[:], in_=ident[:], compare_op=ALU.not_equal, fill=1.0, base=0,
                                    pattern=[[-1, P]], channel_multiplier=1).then_inc(ident_made, 1)
            step.link(nc.gpsimd.memset(ones[:], 1.0))
            step.link(nc.gpsimd.memset(causal[:], 0.0))
            step.link(nc.gpsimd.affine_select(out=causal[:], in_=causal[:], compare_op=ALU.is_ge, fill=NEG, base=0,
                                              pattern=[[-1, P]], channel_multiplier=1))
            step.link(nc.gpsimd.memset(own[:], 0.0))
            step.link(nc.gpsimd.memset(latnew[:], 1.0))
            nc.gpsimd.affine_select(out=own[:], in_=own[:], compare_op=ALU.is_equal, fill=NEG, base=0,
                                    pattern=[[-1, DEC], [0, H]], channel_multiplier=1).then_inc(consts_made, 1)

        def start_pe(pe):
            pe.wait_ge(ident_made, 1)
            pe.wait_ge(consts_made, 1)
            pe.wait_ge(x_in, 16 * (QT + 1 + 6 + CONV))
            nc.tensor.transpose(ps[:, 7, 0:72], gain_rows[:], ident[0:72, 0:72]).then_inc(gains_T, 1)
            for k in range(KD):
                s = k % 4
                if k == 3:
                    pe.wait_ge(gains_made, 1)
                if k >= 4:
                    pe.wait_ge(x_ready, k - 3)
                for t in range(QT):
                    nc.tensor.transpose(ps[:, 2 * s, t * P:(t + 1) * P], x_nat[:, t, k * P:(k + 1) * P], ident[:])
                nc.tensor.transpose(ps[:, 2 * s + 1, 0:DEC], xs_nat[:, k * P:(k + 1) * P],
                                    ident[0:DEC, 0:DEC]).then_inc(xt_made, 1)

        def start_act(act):
            act.wait_ge(gains_made, 1)
            for k in range(KD):
                publish_act(act, 0, k)
                if k < 2:
                    split_hi(act, Unit(k))

        def start_dve(dve):
            nc.vector.memset(acc[:], 0.0).then_inc(acc_cleared, 1)
            dve.wait_ge(gains_T, 1)
            nc.vector.tensor_copy(gain[:], ps[:, 7, 0:72]).then_inc(gains_made, 1)
            dve.wait_ge(gains_made, 1)
            for k in range(KD):
                dve.wait_ge(xt_made, k + 1)
                s = k % 4
                nc.vector.tensor_copy(xT[:, k * T + DEC:(k + 1) * T], ps[:, 2 * s, :])
                nc.vector.tensor_copy(xT[:, k * T:k * T + DEC], ps[:, 2 * s + 1, 0:DEC]).then_inc(x_ready, 1)
                publish_dve(dve, 0, k)
                if k < 2:
                    split_lo(dve, Unit(k))

        STORES = 3 * ("conv" in stages)

        def final_x():
            return KD * (1 + len(stages))

        def end_pe(pe):
            pe.wait_ge(x_ready, final_x())
            for t in range(NT):
                c0, w = col0(t), width(t)
                if t >= 4:
                    for c in y_copied:
                        pe.wait_ge(c, t - 3)
                for k in range(KD):
                    mm = nc.tensor.transpose(ps[0:w, 2 * (t % 4) + k // 4, (k % 4) * P:(k % 4 + 1) * P],
                                             xT[:, k * T + c0:k * T + c0 + w], ident[:])
                    if k % 4 == 3:
                        mm.then_inc(y_turned, 1)

        def end_copy(eng, copy, half):
            for t in range(NT):
                w = width(t)
                if t >= 2:
                    eng.wait_ge(y_out[t % 2], 16 * (t // 2))
                eng.wait_ge(y_turned, 2 * t + half + 1)
                copy(y_nat[0:w, t % 2, half * 512:(half + 1) * 512], ps[0:w, 2 * (t % 4) + half, :]).then_inc(y_copied[half], 1)

        def end_sp(sp):
            for t in range(NT):
                for c in y_copied:
                    sp.wait_ge(c, t + 1)
                dst = (out["y_prompt"][0, t * P:(t + 1) * P, :] if t < QT
                       else out["y_sample"].rearrange("b o d -> (b o) d"))
                sp.dma_start(dst, y_nat[0:width(t), t % 2, :]).then_inc(y_out[t % 2], 16)
            sp.wait_ge(y_out[0], 48)
            sp.wait_ge(y_out[1], 32)
            if STORES:
                sp.wait_ge(stores, 16 * STORES)

        FFN_AT = {int(s[-1]): k for k, s in enumerate([s for s in stages if s[:3] == "ffn"])}
        block = ctx.enter_context(nc.Block())

        @block.sync
        def _(sp):
            start_sp(sp)
            for s, u0 in plan:
                if s[:3] == "ffn":
                    ffn_sp(sp, int(s[-1]), u0)
                elif s == "mla":
                    mla_sp(sp, u0)
                elif s == "conv":
                    conv_sp(sp, u0)
            end_sp(sp)

        @block.gpsimd
        def _(pool):
            start_pool(pool)
            if "mla" in stages:
                decode_pool(pool)

        @block.tensor
        def _(pe):
            start_pe(pe)
            for s, u0 in plan:
                if s[:3] == "ffn":
                    ffn_pe(pe, int(s[-1]), u0)
                elif s == "mla":
                    mla_pe(pe, u0)
                elif s == "conv":
                    conv_pe(pe, u0)
            end_pe(pe)

        @block.scalar
        def _(act):
            start_act(act)
            for s, u0 in plan:
                if s[:3] == "ffn":
                    ffn_act(act, int(s[-1]), u0)
                elif s == "mla":
                    mla_act(act, u0)
                elif s == "conv":
                    conv_act(act, u0)
            end_copy(act, nc.scalar.copy, 1)

        @block.vector
        def _(dve):
            step = Chain(dve, dve_step)
            start_dve(dve)
            for s, u0 in plan:
                if s[:3] == "ffn":
                    ffn_dve(dve, int(s[-1]), u0)
                elif s == "mla":
                    mla_dve(dve, u0, step)
                elif s == "conv":
                    conv_dve(dve, u0, step)
            end_copy(dve, nc.vector.tensor_copy, 0)


_INS = ["x_prompt", "x_sample", "cache_latent", "cache_krope", "state_conv", "page_table",
        "norm_ffn1", "w_ffn1_gate", "w_ffn1_up", "w_ffn1_down", "norm_mix", "norm_ffn2",
        "w_ffn2_gate", "w_ffn2_up", "w_ffn2_down", "w_dq", "q_a_norm", "w_uq", "w_dkv", "kv_a_norm",
        "q_norm", "k_norm", "w_uk", "w_uv", "w_o_attn", "w_conv_in", "conv_w", "w_conv_out"]
_OUTS = [("y_prompt", (1, SEQ, D)), ("y_sample", (DEC, 1, D)),
         ("latent_prompt", (1, SEQ, CL)), ("krope_prompt", (1, SEQ, ROPE)), ("conv_prompt", (1, CONV - 1, D)),
         ("latent_sample", (DEC, 1, CL)), ("krope_sample", (DEC, 1, ROPE)), ("conv_sample", (DEC, CONV - 1, D))]


def rope_tables():
    freq = THETA ** (-np.arange(RH) / RH)
    pos = np.concatenate([np.arange(SEQ), np.full(P, PAST)]).astype(np.float32)
    ang = (pos[:, None] * freq[None, :].astype(np.float32)).astype(np.float32)
    lay = lambda t: np.ascontiguousarray(t.reshape(NT, P, RH).transpose(1, 0, 2)).astype(np.float32)
    return lay(np.cos(ang)), lay(np.sin(ang))


def prepare(nc, inputs, stages=None):
    arrays, a, out = {}, {}, {}
    given = {n: inputs[n] for n in _INS}
    given["rope_cos"], given["rope_sin"] = rope_tables()
    for name, value in given.items():
        value = np.ascontiguousarray(value)
        arrays[f"in_{name}"] = value
        a[name] = nc.dram_tensor(f"in_{name}", value.shape, mybir.dt.from_np(value.dtype), kind="ExternalInput").ap()
    for name, shape in _OUTS:
        out[name] = nc.dram_tensor(f"out_{name}", shape, F32, kind="ExternalOutput").ap()
    if stages is None:
        build(nc, a, out)
    else:
        build(nc, a, out, stages)
    return arrays


def kernel(**inputs):
    import concourse.bacc as bacc
    from concourse.bass_utils import run_bass_kernel_spmd

    nc = bacc.Bacc("TRN2", target_bir_lowering=False, num_devices=1)
    arrays = prepare(nc, inputs)
    got = run_bass_kernel_spmd(nc, [arrays], core_ids=[0]).results[0]
    return tuple(got[f"out_{name}"] for name, _ in _OUTS)
```
